# Optimizing a Trainium2 kernel written in Bass

```python
import math
import jax, jax.numpy as jnp
from jax import lax
import numpy as np

D_MODEL = 1024
BATCH = 1
SEQ = 512
DEPTH = 2
DEC_BATCH = 1
DEC_SEQ = 64
PAST_LEN = 256

CHUNK = 64
QBLK = 128
HEAD_DIM = 64
N_HEADS = D_MODEL // 128
BRANCH_W = N_HEADS * HEAD_DIM
N_BRANCH = 3
N_IDX = 4
IDX_DIM = 64
TOPK_MAX = 256
ROT_DIM = HEAD_DIM // 4
ROPE_THETA = 500000.0
D_FF = ((8 * D_MODEL // 3 + 255) // 256) * 256
CONV_W = 3
FORGET_BIAS = 2.0
EPS = 1e-6
NEG = -1e30
IN_SIZES = (BRANCH_W, HEAD_DIM, HEAD_DIM, N_IDX * IDX_DIM, IDX_DIM, N_IDX,
            BRANCH_W, BRANCH_W, BRANCH_W,
            BRANCH_W, BRANCH_W, BRANCH_W, N_HEADS)
IN_W = sum(IN_SIZES)

kernel_name = 'hybrid_stream_encoder_dsa_stickbreak_fox_step'

def rmsnorm(x, g):
    xf = x.astype(jnp.float32)
    y = xf * lax.rsqrt(jnp.mean(xf * xf, axis=-1, keepdims=True) + EPS)
    return (y * g.astype(jnp.float32)).astype(x.dtype)

def rope(x, pos):
    half = ROT_DIM // 2
    freq = ROPE_THETA ** (-jnp.arange(half, dtype=jnp.float32) / half)
    ang = pos.astype(jnp.float32)[:, None] * freq[None, :]
    shape = (1, pos.shape[0]) + (1,) * (x.ndim - 3) + (half,)
    cos = jnp.cos(ang).reshape(shape)
    sin = jnp.sin(ang).reshape(shape)
    xr = x[..., :ROT_DIM].astype(jnp.float32)
    x1, x2 = xr[..., :half], xr[..., half:]
    rot = jnp.concatenate([x1 * cos - x2 * sin, x2 * cos + x1 * sin], axis=-1).astype(x.dtype)
    return jnp.concatenate([rot, x[..., ROT_DIM:]], axis=-1)

def sweep_queries(fn, q_pos, *q_arrays):
    T = q_pos.shape[0]
    if T <= QBLK:
        return fn(q_pos, *q_arrays)
    nb = T // QBLK
    def split(a):
        return jnp.moveaxis(a.reshape((a.shape[0], nb, QBLK) + a.shape[2:]), 1, 0)
    out = lax.map(lambda args: fn(*args), (q_pos.reshape(nb, QBLK),) + tuple(split(a) for a in q_arrays))
    out = jnp.moveaxis(out, 0, 1)
    return out.reshape((out.shape[0], T) + out.shape[3:])

def dsa_block(q_pos, q, qi, wi, k, v, ki, k_pos, topk):
    f32 = jnp.float32
    dots = jnp.einsum('bqhd,bkd->bqhk', qi.astype(f32), ki.astype(f32)) * IDX_DIM ** -0.5
    score = jnp.einsum('bqhk,bqh->bqk', jax.nn.relu(dots), wi.astype(f32))
    adm = (k_pos[None, :] // CHUNK) <= (q_pos[:, None] // CHUNK)
    score = jnp.where(adm[None], score, NEG)
    top_val, top_idx = lax.top_k(score, topk)
    valid = top_val > 0.5 * NEG
    gather = jax.vmap(lambda rows, idx: rows[idx])
    kg = gather(k, top_idx).astype(f32)
    vg = gather(v, top_idx).astype(f32)
    s = jnp.einsum('bqhd,bqkd->bhqk', q.astype(f32), kg) * HEAD_DIM ** -0.5
    s = jnp.where(valid[:, None], s, NEG)
    p = jax.nn.softmax(s, axis=-1)
    return jnp.einsum('bhqk,bqkd->bqhd', p, vg).astype(q.dtype)

def sb_block(q_pos, q, k, v, k_pos):
    f32 = jnp.float32
    z = jnp.einsum('bqhd,bkhd->bhqk', q.astype(f32), k.astype(f32)) * HEAD_DIM ** -0.5
    strict = k_pos[None, :] < q_pos[:, None]
    la = jnp.where(strict, jax.nn.log_sigmoid(-z), 0.0)
    after = lax.cumsum(la, axis=3, reverse=True) - la
    a = jnp.where(strict, jnp.exp(jax.nn.log_sigmoid(z) + after), 0.0)
    return jnp.einsum('bhqk,bkhd->bqhd', a, v.astype(f32)).astype(q.dtype)

def fox_block(q_pos, q, fq, k, v, fk, k_pos):
    f32 = jnp.float32
    s = jnp.einsum('bqhd,bkhd->bhqk', q.astype(f32), k.astype(f32)) * HEAD_DIM ** -0.5
    s = s + jnp.moveaxis(fq, 1, 2)[:, :, :, None] - jnp.moveaxis(fk, 1, 2)[:, :, None, :]
    causal = k_pos[None, :] <= q_pos[:, None]
    p = jax.nn.softmax(jnp.where(causal, s, NEG), axis=-1)
    return jnp.einsum('bhqk,bkhd->bqhd', p, v.astype(f32)).astype(q.dtype)

def token_mix(xn, past, w_in, b_f, w_branch, w_gate, w_out):
    B, T, _ = xn.shape
    L = T if past is None else past[0].shape[1] + T
    pos = jnp.arange(L - T, L)
    points = np.cumsum(IN_SIZES)[:-1].tolist()
    (a_q, a_k, a_v, i_q, i_k, i_w, b_q, b_k, b_v, c_q, c_k, c_v, c_f) = jnp.split(xn @ w_in, points, axis=-1)
    heads = lambda t: t.reshape(B, T, N_HEADS, HEAD_DIM)
    a_q = rope(heads(a_q), pos)
    a_k = rope(a_k, pos)
    i_q = rope(i_q.reshape(B, T, N_IDX, IDX_DIM), pos)
    i_k = rope(i_k, pos)
    i_w = i_w * N_IDX ** -0.5
    b_q, b_k, b_v = heads(b_q), heads(b_k), heads(b_v)
    c_q, c_k, c_v = heads(c_q), heads(c_k), heads(c_v)
    c_logf = jax.nn.log_sigmoid(c_f.astype(jnp.float32) + b_f.astype(jnp.float32))
    new_rows = (a_k, a_v, i_k, b_k, b_v, c_k, c_v, c_logf)
    if past is None:
        ka, va, kia, kb, vb, kc, vc, logf = new_rows
    else:
        ka, va, kia, kb, vb, kc, vc, logf = (jnp.concatenate([p_, n_], axis=1) for p_, n_ in zip(past, new_rows))
    k_pos = jnp.arange(L)
    topk = max(1, min(TOPK_MAX, L // 4))
    fk = jnp.cumsum(logf.astype(jnp.float32), axis=1)
    fq = fk[:, L - T:]
    o_a = sweep_queries(lambda qp, q, qi, wi: dsa_block(qp, q, qi, wi, ka, va, kia, k_pos, topk), pos, a_q, i_q, i_w)
    o_b = sweep_queries(lambda qp, q: sb_block(qp, q, kb, vb, k_pos), pos, b_q)
    o_c = sweep_queries(lambda qp, q, f: fox_block(qp, q, f, kc, vc, fk, k_pos), pos, c_q, fq)
    o = jnp.stack([o_a, o_b, o_c], axis=2).reshape(B, T, N_BRANCH, BRANCH_W)
    branch = jnp.einsum('btnw,nwd->btnd', o, w_branch)
    gate = jax.nn.sigmoid((xn @ w_gate).reshape(B, T, N_BRANCH, D_MODEL))
    return jnp.einsum('btnd,btnd->btd', gate, branch) @ w_out, new_rows

def conv_ffn(xn, conv_past, w_up, conv_w, conv_b, w_down):
    T = xn.shape[1]
    h = xn @ w_up
    hp = jnp.concatenate([conv_past.astype(h.dtype), h], axis=1)
    hc = conv_b + conv_w[0] * hp[:, 0:T]
    for i in range(1, CONV_W):
        hc = hc + conv_w[i] * hp[:, i:i + T]
    g, u = jnp.split(hc, 2, axis=-1)
    return (jax.nn.silu(g) * u) @ w_down, hp[:, -(CONV_W - 1):]

def trunk(x, past, norm_mix, w_in, b_f, w_branch, w_gate, w_out, norm_ffn, w_up, conv_w, conv_b, w_down, norm_final):
    per_layer = []
    for l in range(DEPTH):
        lp = None if past is None else tuple(c[l] for c in past[:-1])
        m, rows = token_mix(rmsnorm(x, norm_mix[l]), lp, w_in[l], b_f[l], w_branch[l], w_gate[l], w_out[l])
        x = x + m
        if past is None:
            conv_past = jnp.zeros((x.shape[0], CONV_W - 1, 2 * D_FF), x.dtype)
        else:
            conv_past = past[-1][l]
        f, conv_state = conv_ffn(rmsnorm(x, norm_ffn[l]), conv_past, w_up[l], conv_w[l], conv_b[l], w_down[l])
        x = x + f
        per_layer.append(rows + (conv_state,))
    new_state = tuple(jnp.stack(s, axis=0) for s in zip(*per_layer))
    return rmsnorm(x, norm_final), new_state

def setup_inputs(seed: int = 0) -> dict:
    key = jax.random.key(seed)
    ks = jax.random.split(key, 24)
    f32 = jnp.float32
    nrm = lambda k, shape, scale=1.0: scale * jax.random.normal(k, shape, f32)
    F2 = 2 * D_FF
    return {
        'x_prompt': nrm(ks[0], (BATCH, SEQ, D_MODEL)),
        'x_sample': nrm(ks[1], (DEC_BATCH, DEC_SEQ, D_MODEL)),
        'cache_a_k': nrm(ks[2], (DEPTH, DEC_BATCH, PAST_LEN, HEAD_DIM)),
        'cache_a_v': nrm(ks[3], (DEPTH, DEC_BATCH, PAST_LEN, HEAD_DIM)),
        'cache_a_idx_k': nrm(ks[4], (DEPTH, DEC_BATCH, PAST_LEN, IDX_DIM)),
        'cache_b_k': nrm(ks[5], (DEPTH, DEC_BATCH, PAST_LEN, N_HEADS, HEAD_DIM)),
        'cache_b_v': nrm(ks[6], (DEPTH, DEC_BATCH, PAST_LEN, N_HEADS, HEAD_DIM)),
        'cache_c_k': nrm(ks[7], (DEPTH, DEC_BATCH, PAST_LEN, N_HEADS, HEAD_DIM)),
        'cache_c_v': nrm(ks[8], (DEPTH, DEC_BATCH, PAST_LEN, N_HEADS, HEAD_DIM)),
        'cache_c_logf': jax.nn.log_sigmoid(FORGET_BIAS + nrm(ks[9], (DEPTH, DEC_BATCH, PAST_LEN, N_HEADS))),
        'state_ffn_conv': nrm(ks[10], (DEPTH, DEC_BATCH, CONV_W - 1, F2)),
        'norm_mix': 1.0 + nrm(ks[11], (DEPTH, D_MODEL), 0.02),
        'w_in': nrm(ks[12], (DEPTH, D_MODEL, IN_W), D_MODEL ** -0.5),
        'b_f': FORGET_BIAS + nrm(ks[13], (DEPTH, N_HEADS), 0.5),
        'w_branch': nrm(ks[14], (DEPTH, N_BRANCH, BRANCH_W, D_MODEL), BRANCH_W ** -0.5),
        'w_gate': nrm(ks[15], (DEPTH, D_MODEL, N_BRANCH * D_MODEL), D_MODEL ** -0.5),
        'w_out': nrm(ks[16], (DEPTH, D_MODEL, D_MODEL), D_MODEL ** -0.5),
        'norm_ffn': 1.0 + nrm(ks[17], (DEPTH, D_MODEL), 0.02),
        'w_up': nrm(ks[18], (DEPTH, D_MODEL, F2), D_MODEL ** -0.5),
        'conv_w': nrm(ks[19], (DEPTH, CONV_W, F2), CONV_W ** -0.5),
        'conv_b': nrm(ks[20], (DEPTH, F2), 0.02),
        'w_down': nrm(ks[21], (DEPTH, D_FF, D_MODEL), D_FF ** -0.5),
        'norm_final': 1.0 + nrm(ks[22], (D_MODEL,), 0.02),
    }

def reference(x_prompt, x_sample, cache_a_k, cache_a_v, cache_a_idx_k, cache_b_k, cache_b_v, cache_c_k, cache_c_v,
              cache_c_logf, state_ffn_conv, norm_mix, w_in, b_f, w_branch, w_gate, w_out, norm_ffn, w_up, conv_w,
              conv_b, w_down, norm_final):
    weights = (norm_mix, w_in, b_f, w_branch, w_gate, w_out, norm_ffn, w_up, conv_w, conv_b, w_down, norm_final)
    y_prompt, (p_a_k, p_a_v, p_a_idx_k, p_b_k, p_b_v, p_c_k, p_c_v, p_c_logf, p_ffn_conv) = trunk(x_prompt, None, *weights)
    past = (cache_a_k, cache_a_v, cache_a_idx_k, cache_b_k, cache_b_v, cache_c_k, cache_c_v, cache_c_logf, state_ffn_conv)
    y_sample, (s_a_k, s_a_v, s_a_idx_k, s_b_k, s_b_v, s_c_k, s_c_v, s_c_logf, s_ffn_conv) = trunk(x_sample, past, *weights)
    return (y_prompt, y_sample, p_a_k, p_a_v, p_a_idx_k, p_b_k, p_b_v, p_c_k, p_c_v, p_c_logf, p_ffn_conv,
            s_a_k, s_a_v, s_a_idx_k, s_b_k, s_b_v, s_c_k, s_c_v, s_c_logf, s_ffn_conv)


_drawn_inputs = setup_inputs


def setup_inputs(seed=0):
    import zlib

    import numpy as np

    out = dict(_drawn_inputs(seed))
    spreads = {}
    factors = {}
    for name, (base, spread) in spreads.items():
        noise = np.random.default_rng([zlib.crc32(name.encode()), seed]).standard_normal(out[name].shape)
        drawn = base * np.exp(spread * noise) if base else spread * noise
        out[name] = __import__('jax').numpy.asarray(drawn.astype(out[name].dtype))
    for name, factor in factors.items():
        out[name] = (out[name] * factor).astype(out[name].dtype)
    return out
```

```python
from contextlib import ExitStack

import concourse.bass as bass
from concourse import mybir

F32 = mybir.dt.float32
F32R = mybir.dt.float32r
BF16 = mybir.dt.bfloat16
ALU = mybir.AluOpType
ACT = mybir.ActivationFunctionType
AX_X = mybir.AxisListType.X

P = 128
D_MODEL = 1024
KD = D_MODEL // P
LAYERS = 2
TP = 512
TS = 64
T = TP + TS
HALF = T // 2
PAST = 256
KEYS = T + PAST
HD = 64
HEADS = 8
IDX_HEADS = 4
D_FF = 2816
FT = D_FF // P
FH = FT // 2
CONV = 3
EPS = 1e-6
NEG = -1e30
TAKEN = -3e38
TOPK_P = 128
TOPK_S = 80
ROT = 16
SMALL = HD + IDX_HEADS + HEADS
QT = TP // P

U_KI, U_IQ, U_SMALL = 0, 1, 3
B, C, A = 0, 1, 2
U_Q = {B: 4, C: 28, A: 52}
U_K = {B: 8, C: 32}
U_V = {B: 12, C: 36}
U_G = {B: 16, C: 40, A: 56}
U_BR = {B: 24, C: 48, A: 64}
U_OUT = 68
U_UP = 76
U_DOWN = U_UP + 2 * FH
U_HALF = 2 * FH + 12
UNITS = U_UP + 2 * U_HALF
CHUNKS = 2 * UNITS
SPLIT_SLOTS = 4
RAW_SLOTS = 2

D_NORM1, D_KI, D_IQ0, D_PKI, D_IQ1, D_PIQ0, D_PIQ1 = range(7)
D_Q = {B: 7, C: 32}
D_K = {B: 11, C: 36}
D_V = {B: 15, C: 40}
D_G = {B: 16, C: 41, A: 65}
D_BR = {B: 24, C: 49, A: 73}
D_AQ, D_AP = (57, 58, 60, 62), (59, 61, 63, 64)
D_OUT = 81
D_NORM2 = 89
D_UP = 90
D_DOWN = D_UP + 2 * FH
D_HALF = 2 * FH + KD
D_USES = D_UP + 2 * D_HALF
assert UNITS % RAW_SLOTS == 0 and CHUNKS % SPLIT_SLOTS == 0 and D_USES % 2 == 0

C_ID, C_NTRI, C_NONE, C_ONE, C_ROT, C_COS, C_SIN, C_END = 0, 128, 256, 384, 512, 640, 640 + T, 640 + 2 * T
M_ID, M_SB, M_SBN, M_CA, M_CAN, M_SEL, M_END = 0, 128, 256, 320, 448, 576, 576 + HEADS * P
R_GM = 0
R_GF = R_GM + LAYERS * KD
R_GE = R_GF + LAYERS * KD
R_BF = R_GE + KD
R_CW = R_BF + LAYERS
R_CB = R_CW + LAYERS * 2 * FT * CONV
R_SS = R_CB + LAYERS * 2 * FT
R_END = R_SS + LAYERS * 2 * FT * 2

B_COLS = (512, 512, 448)
S_SEG = ((0, 512), (512, 1024), (1024, 1280), (1280, 1664))
I_SEG = ((0, 512, 640), (512, 896, 256), (896, 1152, 0))
I_QT = (3, 2, 1)

DVE_STRIDE, ACT_STRIDE, POOL_STRIDE = 1024, 512, 128


def encoder(nc, xT, w, const, masks, par, ki_past, v_past, bc_k_past, bc_v_past, lf_past,
            y, o_ki, o_k, o_v, o_av, o_lf, o_conv):
    with ExitStack() as ctx:
        def sb(name, shape, dt=F32):
            return ctx.enter_context(nc.sbuf_tensor(name, shape, dt))

        def shared(*groups):
            made, size = [], 0
            for group in groups:
                with ExitStack() as stage:
                    made += [stage.enter_context(nc.sbuf_tensor(n, s, d)) for n, s, d in group]
                words = 0
                for _, s, d in group:
                    n = 1
                    for m in s[1:]:
                        n *= m
                    words += n
                size = max(size, words)
            sb(groups[0][0][0] + "_space", [P, size])
            return made

        x = sb("x", [P, KD, T])
        xh = sb("xh", [P, KD, T], F32R)
        xl = sb("xl", [P, KD, T], F32R)
        q, k, v, g, _, oh, _, ol, ah, al = shared(
            [("q", [P, 4, T], F32), ("k", [P, 4, KEYS], F32), ("v", [P, 7, HEADS * HD], F32),
             ("g", [P, KD, T], F32)],
            [("over_q", [P, 4 * T], F32), ("oh", [P, 4, T], F32R), ("rest_of_k", [P, 4 * PAST], F32),
             ("ol", [P, 4, T], F32R)],
            [("ah", [P, FH, T], F32R), ("al", [P, FH, T], F32R)])
        k2 = sb("k2", [P, 2, KEYS])
        av = sb("av", [P, 7, HD])
        z = sb("z", [P, KD, T])
        w1, w2, _, iq, hb, cv, at = shared(
            [("w1", [P, 1664], F32), ("w2", [P, 2240], F32)],
            [("over_w1", [P, 1664], F32), ("iq", [P, 2, T], F32)],
            [("hb", [P, 2, T + 4], F32), ("cv", [P, 2, T + 2], F32), ("at", [P, T], F32)])
        scores = sb("scores", [P, 1152])
        scores_s = sb("scores_s", [TS, PAST + TS])
        chosen = sb("chosen", [P, 1664], BF16)
        top8 = sb("top8", [P, 4, 8])
        raw = [sb(f"raw{i}", [P, 1024]) for i in range(RAW_SLOTS)]
        wh = sb("wh", [P, SPLIT_SLOTS, 512], F32R)
        wl = sb("wl", [P, SPLIT_SLOTS, 512], F32R)
        tmp = sb("tmp", [P, 2, T])
        rstd = sb("rstd", [P, T])
        sumsq = sb("sumsq", [P, T])
        cf = sb("cf", [P, C_END])
        cb = sb("cb", [P, M_END], BF16)
        pr = sb("pr", [P, R_END])
        fparts = sb("fparts", [P, KEYS], BF16)
        conv_out = sb("conv_out", [P, 2 * FT, 4])
        wi = sb("wi", [P, 5, IDX_HEADS])
        cfg = sb("cfg", [P, 5, HEADS])
        nm = sb("nm", [P, 5])
        rs = sb("rs", [P, 5])
        ri = sb("ri", [P, 5])
        eps = sb("eps", [P, 1])

        ki = z[:, 7, :]
        zf = z[:].rearrange("p a b -> p (a b)")
        ly, lt, spf, lfo = z[0:HEADS, 0, :], z[0:HEADS, 1, :], z[0:HEADS, 2, :], z[0:HEADS, 3, :]
        clf, one8, nf = zf[0:HEADS, 4 * T:4 * T + PAST], zf[0:HEADS, 2600:2600 + TP], zf[0:HEADS, 3136:3136 + KEYS]
        part16 = zf[0:HEADS, 4 * T:4 * T + KEYS // 2].bitcast(BF16)

        dbank = [ctx.enter_context(nc.psum_tensor(f"d{i}", [P, 1024], F32)) for i in range(2)]
        ab = ctx.enter_context(nc.psum_tensor("ab", [P, 4, 512], F32))
        dv = [d[:, 512 - HALF:512 + HALF] for d in dbank]
        dhalf = [[d[:, 512 - HALF:512], d[:, 512:512 + HALF]] for d in dbank]

        def sem(name):
            return ctx.enter_context(nc.semaphore(name))

        carrier = sem("carrier")
        s_x, s_const, s_bf = sem("s_x"), sem("s_const"), sem("s_bf")
        landed = [sem(f"landed{i}") for i in range(RAW_SLOTS)]
        high_done, low_done, chunks = sem("high_done"), sem("low_done"), sem("chunks")
        dfree = [sem("dfree0"), sem("dfree1")]
        perms, norms, acc_ready, rstd_ready, xt_ready, xh_ready, xl_ready = map(sem, (
            "perms", "norms", "acc_ready", "rstd_ready", "xt_ready", "xh_ready", "xl_ready"))
        roped = sem("roped")
        past_i, past_b, past_c = sem("past_i"), sem("past_b"), sem("past_c")
        v_ready, small_ready = sem("v_ready"), sem("small_ready")
        logf_mm, ly_ready, lt_ready, logf_ready, fparts_ready = map(sem, (
            "logf_mm", "ly_ready", "lt_ready", "logf_ready", "fparts_ready"))
        dots, relus, idx_added, chosen_ready = map(sem, ("dots", "relus", "idx_added", "chosen_ready"))
        zs, soft, sps, sufs, atts = map(sem, ("zs", "soft", "sps", "sufs", "atts"))
        ss, maxes, exps, scaled, turned, pts = map(sem, ("ss", "maxes", "exps", "scaled", "turned", "pts"))
        pvs, o_ready, o_split, gates_ready = map(sem, ("pvs", "o_ready", "o_split", "gates_ready"))
        z_ready = sem("z_ready")
        hb_ready, conv_done, silu_done, act_ready, ah_ready, al_ready = map(sem, (
            "hb_ready", "conv_done", "silu_done", "act_ready", "ah_ready", "al_ready"))
        st_ki, st_k, st_v, st_small, st_lf, st_conv, st_y = map(sem, (
            "st_ki", "st_k", "st_v", "st_small", "st_lf", "st_conv", "st_y"))
        conv_rows, y_ready = sem("conv_rows"), sem("y_ready")
        dve_steps, act_steps, pool_steps = sem("dve_steps"), sem("act_steps"), sem("pool_steps")

        def chunks_done(l, n):
            return l * CHUNKS + SPLIT_SLOTS + n

        def freed(l, d):
            return l * (D_USES // 2) + d // 2

        def wait_taken(eng, l, d):
            eng.wait_ge(dfree[d % 2], freed(l, d) + 1)

        def apart(eng):
            eng.sem_inc(carrier, 1)

        ident, identb = cf[:, C_ID:C_ID + P], cb[:, M_ID:M_ID + P]

        def tile_keys(t):
            return (t + 1) * P

        block = ctx.enter_context(nc.Block())

        @block.sync
        def _(sp):
            sp.dma_start(raw[0][:], w[0]).then_inc(landed[0], 16)
            sp.dma_start(cf[:], const).then_inc(s_const, 16)
            sp.dma_start(pr[:], par).then_inc(s_const, 16)
            sp.dma_start(x[:], xT).then_inc(s_x, 16)
            sp.dma_start(w1[:, 0:M_END], masks).then_inc(s_const, 16)
            sp.dma_start(raw[1][:], w[1]).then_inc(landed[1], 16)
            with sp.Fori(1, (LAYERS * UNITS + 2) // 2) as pair:
                for s in range(2):
                    sp.wait_ge(low_done, 4 * pair + 2 * s - 2)
                    sp.dma_start(raw[s][:], w[bass.ds(2 * pair + s, 1)].rearrange("a p n -> (a p) n"))\
                      .then_inc(landed[s], 16)

        @block.gpsimd
        def _(pool):
            n = [0]

            def square(j, base, ready=None):
                if j == 0:
                    pool.tensor_tensor(sumsq[:], x[:, 0, :], x[:, 0, :], ALU.mult).then_inc(pool_steps, 1)
                    n[0] += 1
                    return
                if j > 1:
                    pool.wait_ge(pool_steps, base + n[0])
                pool.tensor_tensor(rstd[:], x[:, j, :], x[:, j, :], ALU.mult).then_inc(pool_steps, 1)
                n[0] += 1
                pool.wait_ge(pool_steps, base + n[0])
                last = pool.tensor_tensor(sumsq[:], sumsq[:], rstd[:], ALU.add)
                last.then_inc(acc_ready if j == KD - 1 else pool_steps, 1)
                if j < KD - 1:
                    n[0] += 1

            def low_parts(l, r):
                for kk in range(KD):
                    pool.wait_ge(xh_ready, l * 3 * KD + r * KD + kk + 1)
                    src = z[:, kk, :] if r == 1 else tmp[:, kk % 2, :]
                    pool.tensor_tensor(xl[:, kk, :], src, xh[:, kk, :].bitcast(F32), ALU.subtract).then_inc(xl_ready, 1)

            pool.wait_ge(s_x, 16)
            for j in range(KD):
                square(j, 0)
            first = n[0]
            with pool.Fori(0, LAYERS) as l:
                n[0] = 0
                base = l * POOL_STRIDE + first
                low_parts(l, 0)
                pool.wait_ge(roped, l * 8 + 1)
                pool.dma_start(o_ki[bass.ds(l, 1)].rearrange("a p n -> (a p) n"), ki).then_inc(st_ki, 16)
                pool.wait_ge(small_ready, l + 1)
                pool.dma_start(o_av[bass.ds(l, 1), 0:TP, :].rearrange("a (t p) n -> (a p) t n", p=P), av[:, 0:4, :]).then_inc(st_small, 16)
                pool.dma_start(o_av[bass.ds(l, 1), TP:T, :].rearrange("a p n -> (a p) n"), av[0:TS, 4, :]).then_inc(st_small, 16)
                pool.wait_ge(logf_ready, l + 1)
                pool.dma_start(o_lf[bass.ds(l, 1)].rearrange("a p n -> (a p) n"), lfo).then_inc(st_lf, 16)
                for m in (B, C):
                    for j in (2, 3):
                        wait_taken(pool, l, D_K[m] + j)
                    pool.dma_start(o_k[bass.ds(2 * l + m, 1)].rearrange("a p t n -> (a p) t n"), k[:, :, 0:T]).then_inc(st_k, 16)
                    pool.wait_ge(v_ready, l * 2 + m + 1)
                    apart(pool)
                    ov = o_v[bass.ds(2 * l + m, 1)]
                    pool.dma_start(ov[:, 0:TP, :].rearrange("a (t p) n -> (a p) t n", p=P), v[:, 0:4, :]).then_inc(st_v, 16)
                    pool.dma_start(ov[:, TP:T, :].rearrange("a p n -> (a p) n"), v[0:TS, 4, :]).then_inc(st_v, 16)
                low_parts(l, 1)
                for j in range(KD):
                    wait_taken(pool, l, D_OUT + j)
                    square(j, base)
                low_parts(l, 2)
                per_half = n[0]
                outer = base + n[0]
                with pool.Fori(0, 2) as f:
                    with pool.Fori(0, FH) as i:
                        pool.wait_ge(ah_ready, l * FT + f * FH + i + 1)
                        pool.tensor_tensor(al[:, bass.ds(i, 1), :].rearrange("p a n -> p (a n)"), at[:],
                                           ah[:, bass.ds(i, 1), :].rearrange("p a n -> p (a n)").bitcast(F32),
                                           ALU.subtract).then_inc(al_ready, 1)
                    n[0] = 0
                    for j in range(KD):
                        d = D_DOWN + j
                        pool.wait_ge(dfree[d % 2], freed(l, d) + 1 + f * (D_HALF // 2))
                        square(j, outer + f * per_half)
                assert n[0] == per_half
                pool.wait_ge(pool_steps, base + 3 * per_half)
                pool.sem_inc(pool_steps, POOL_STRIDE - 3 * per_half)
                pool.wait_ge(conv_rows, (l + 1) * 2 * FT)
                pool.dma_start(o_conv[bass.ds(l, 1)].rearrange("a p t n -> (a p) t n"), conv_out[:]).then_inc(st_conv, 16)
            for j in range(KD):
                pool.wait_ge(y_ready, j + 1)
                pool.dma_start(y[:, j, :], z[:, j, :]).then_inc(st_y, 16)
            for s, count in ((st_ki, LAYERS), (st_small, 2 * LAYERS), (st_lf, LAYERS), (st_k, 2 * LAYERS),
                             (st_v, 4 * LAYERS), (st_conv, LAYERS), (st_y, KD)):
                pool.wait_ge(s, 16 * count)

        @block.scalar
        def _(act):
            steps = [0]
            split = [0]

            def high_parts(l, upto, at_chunk=None):
                while split[0] <= upto:
                    c = split[0]
                    high_part(l * CHUNKS, l * (UNITS // 2), c)
                    split[0] += 1

            def high_part(before, units_before, c):
                v_ = c // 2
                if c % 2 == 0:
                    act.wait_ge(landed[v_ % 2], 16 * (units_before + v_ // 2 + 1))
                act.wait_ge(chunks, before + c + 1)
                act.activation(wh[:, c % SPLIT_SLOTS, :], raw[v_ % 2][:, (c % 2) * 512:(c % 2) * 512 + 512],
                               ACT.Copy).then_inc(high_done, 1)

            def rsqrt_of(l, d, src_count, n_norm):
                act.wait_ge(norms, src_count)
                act.activation(rstd[:], dv[d % 2], ACT.Ln, bias=eps[:], scale=1.0 / D_MODEL).then_inc(dfree[d % 2], 1)
                act.wait_ge(dfree[d % 2], freed(l, d) + 1)
                act.activation(rstd[:], rstd[:], ACT.Exp, scale=-0.5).then_inc(rstd_ready, 1)

            def round_x(l, r):
                for kk in range(KD):
                    if r == 1:
                        act.wait_ge(z_ready, l * KD + kk + 1)
                        src = z[:, kk, :]
                    else:
                        act.wait_ge(xt_ready, l * 2 * KD + (r // 2) * KD + kk + 1)
                        src = tmp[:, kk % 2, :]
                    act.activation(xh[:, kk, :], src, ACT.Copy).then_inc(xh_ready, 1)

            def take(l, d, c_last, dst, scale=1.0):
                high_parts(l, c_last + 4)
                act.wait_ge(chunks, chunks_done(l, c_last + 1))
                return act.activation(dst, dv[d % 2], ACT.Copy, scale=scale)

            act.preload_act_table_set("natural_log_exp_and_others")
            act.wait_ge(s_bf, 1)
            for c in range(SPLIT_SLOTS):
                high_part(0, 0, c)
            with act.Fori(0, LAYERS) as l:
                split[0] = SPLIT_SLOTS
                steps[0] = 0
                here = l * ACT_STRIDE
                act.preload_act_table_set("natural_log_exp_and_others")
                rsqrt_of(l, D_NORM1, 2 * l + 1, 0)
                act.dma_start(k2[:, :, T:KEYS], ki_past[bass.ds(l, 1)].rearrange("a p t n -> (a p) t n")).then_inc(past_i, 16)
                act.dma_start(av[:, 5:7, :], v_past[bass.ds(l, 1)].rearrange("a (t p) n -> (a p) t n", p=P)).then_inc(past_i, 16)
                act.dma_start(clf, lf_past[bass.ds(l, 1)].rearrange("a p n -> (a p) n")).then_inc(past_i, 16)
                act.dma_start(k[:, :, T:KEYS], bc_k_past[bass.ds(2 * l, 1)].rearrange("a p t n -> (a p) t n")).then_inc(past_b, 16)
                act.dma_start(v[:, 5:7, :], bc_v_past[bass.ds(2 * l, 1)].rearrange("a (t p) n -> (a p) t n", p=P)).then_inc(past_b, 16)
                round_x(l, 0)
                take(l, D_KI, 1, ki).then_inc(dfree[D_KI % 2], 1)
                take(l, D_IQ0, 3, iq[:, 0, :], 0.125).then_inc(dfree[D_IQ0 % 2], 1)
                take(l, D_IQ1, 5, iq[:, 1, :], 0.125).then_inc(dfree[D_IQ1 % 2], 1)
                high_parts(l, 11)
                act.wait_ge(ly_ready, l + 1)
                act.activation(lt, ly, ACT.Abs).then_inc(act_steps, 1)
                steps[0] += 1
                act.wait_ge(act_steps, here + steps[0])
                act.activation(lt, lt, ACT.Exp, scale=-1.0).then_inc(act_steps, 1)
                steps[0] += 1
                act.wait_ge(act_steps, here + steps[0])
                act.activation(lt, lt, ACT.Ln, bias=1.0).then_inc(lt_ready, 1)

                for m in (B, C, A):
                    if m == C:
                        act.wait_ge(chunks, chunks_done(l, 2 * U_BR[B] + KD))
                        act.dma_start(k[:, :, T:KEYS], bc_k_past[bass.ds(2 * l + 1, 1)].rearrange("a p t n -> (a p) t n")).then_inc(past_c, 16)
                        act.dma_start(v[:, 5:7, :], bc_v_past[bass.ds(2 * l + 1, 1)].rearrange("a (t p) n -> (a p) t n", p=P)).then_inc(past_c, 16)
                    for j in range(4):
                        d = D_AQ[j] if m == A else D_Q[m] + j
                        take(l, d, 2 * U_Q[m] + 2 * j + 1, q[:, j, :], 0.125).then_inc(dfree[d % 2], 1)
                    if m == B:
                        for i in range(IDX_HEADS):
                            for s in range(4):
                                act.wait_ge(dots, l * 16 + 4 * i + s + 1)
                                if i:
                                    act.wait_ge(idx_added, l * 16 + 4 * i + s - 3)
                                if s < 3:
                                    a, b, _ = I_SEG[s]
                                    act.activation(w1[:, a:b], ab[:, s, 0:b - a], ACT.Relu).then_inc(relus, 1)
                                else:
                                    act.activation(w1[0:TS, 1152:1472], ab[0:TS, 3, 0:320], ACT.Relu).then_inc(relus, 1)
                    if m != A:
                        for j in range(4):
                            d = D_K[m] + j
                            take(l, d, 2 * U_K[m] + 2 * j + 1, k[:, j, 0:T]).then_inc(dfree[d % 2], 1)
                        high_parts(l, 2 * U_V[m] + 7 + 4)

                    for h in range(HEADS):
                        n_head = 8 * m + h
                        cg = 2 * U_G[m] + 2 * h
                        if m == B:
                            high_parts(l, cg + 3)
                            t3 = l * 3 * HEADS + 3 * h
                            for b, cols in enumerate(B_COLS):
                                act.wait_ge(zs, t3 + b + 1)
                                if h:
                                    act.wait_ge(sufs, t3)
                                act.activation(w1[:, 512 * b:512 * b + cols], ab[:, b, 0:cols], ACT.Abs).then_inc(act_steps, 1)
                            for b, cols in enumerate(B_COLS):
                                act.wait_ge(act_steps, here + steps[0] + b + 1)
                                act.activation(w1[:, 512 * b:512 * b + cols], w1[:, 512 * b:512 * b + cols], ACT.Exp, scale=-1.0).then_inc(act_steps, 1)
                            steps[0] += 3
                            for b, cols in enumerate(B_COLS):
                                act.wait_ge(act_steps, here + steps[0] + b + 1)
                                act.activation(w1[:, 512 * b:512 * b + cols], w1[:, 512 * b:512 * b + cols], ACT.Ln, bias=1.0).then_inc(soft, 1)
                            steps[0] += 3
                            high_parts(l, cg + 4)
                            for b, cols in enumerate(B_COLS):
                                act.wait_ge(sufs, t3 + b + 1)
                                if h:
                                    act.wait_ge(pvs, l * 24 + n_head)
                                act.activation(w2[:, 512 * b:512 * b + cols], ab[:, b, 0:cols], ACT.Exp).then_inc(atts, 1)
                            take(l, D_G[m] + h, cg + 1, g[:, h, :]).then_inc(dfree[(D_G[m] + h) % 2], 1)
                            continue

                        hh = n_head - 8
                        t4, t3 = l * 64 + 4 * hh, l * 48 + 3 * hh

                        def exp_step(s):
                            act.wait_ge(maxes, t4 + s + 1)
                            if hh:
                                act.wait_ge(turned, t3 - 3 + (1, 2, 3, 3)[s])
                            a, b = S_SEG[s]
                            if s == 0:
                                act.activation(w1[:, 0:128], ab[:, 0, 0:128], ACT.Exp, bias=nm[:, 0:1], accum_out=rs[:, 0:1])
                                last = act.activation(w1[:, 128:512], ab[:, 0, 128:512], ACT.Exp, bias=nm[:, 1:2], accum_out=rs[:, 1:2])
                            elif s == 3:
                                last = act.activation(w1[0:TS, a:b], ab[0:TS, 1, 0:384], ACT.Exp, bias=nm[0:TS, 4:5], accum_out=rs[0:TS, 4:5])
                            else:
                                last = act.activation(w1[:, a:b], ab[:, s % 2, 0:b - a], ACT.Exp, bias=nm[:, s + 1:s + 2], accum_out=rs[:, s + 1:s + 2])
                            last.then_inc(exps, 1)

                        def turn_step(s):
                            act.wait_ge(turned, t3 + s + 1)
                            if s == 0:
                                act.wait_ge(pvs, l * 24 + n_head)
                                act.activation(w2[:, 0:128], ab[:, 2, 0:128], ACT.Copy)
                                last = act.activation(w2[:, 0:1536].rearrange("p (t n) -> p t n", n=512)[:, :, 256:384],
                                                      ab[:, 2, 128:512].rearrange("p (t n) -> p t n", n=P), ACT.Copy)
                            elif s == 1:
                                last = act.activation(w2[:, 0:2048].rearrange("p (t n) -> p t n", n=512)[:, :, 384:512],
                                                      ab[:, 2, :].rearrange("p (t n) -> p t n", n=P), ACT.Copy)
                            else:
                                act.activation(w2[:, 0:1024].rearrange("p (t n) -> p t n", n=512)[:, :, 128:256],
                                               ab[:, 2, 0:256].rearrange("p (t n) -> p t n", n=P), ACT.Copy)
                                last = act.activation(w2[:, 2048:2240], ab[:, 2, 256:448], ACT.Copy)
                            last.then_inc(pts, 1)

                        high_parts(l, cg + 3)
                        exp_step(0)
                        exp_step(1)
                        high_parts(l, cg + 4)
                        exp_step(2)
                        turn_step(0)
                        exp_step(3)
                        turn_step(1)
                        take(l, D_G[m] + h, cg + 1, g[:, h, :]).then_inc(dfree[(D_G[m] + h) % 2], 1)
                        turn_step(2)

                    for j in range(KD):
                        d = D_G[m] + j
                        act.wait_ge(dfree[d % 2], freed(l, d) + 1)
                        act.activation(g[:, j, :], g[:, j, :], ACT.Sigmoid).then_inc(gates_ready, 1)
                    if m != A:
                        act.preload_act_table_set("natural_log_exp_and_others")
                    for j in range(KD):
                        high_parts(l, 2 * U_BR[m] + j + 4)

                round_x(l, 1)
                high_parts(l, 2 * U_OUT + 2 * KD + 3)
                act.preload_act_table_set("natural_log_exp_and_others")
                rsqrt_of(l, D_NORM2, 2 * l + 2, 1)
                round_x(l, 2)

                act.wait_ge(st_conv, 16 * l)
                with act.Fori(0, 2) as f:
                    with act.Fori(0, FH) as i:
                        before = l * CHUNKS + f * (2 * U_HALF) + 4 * i
                        units_before = l * (UNITS // 2) + f * (U_HALF // 2) + i
                        pair = l * FT + f * FH + i
                        for s in range(2):
                            for c in (2 * U_UP + 4 + 2 * s, 2 * U_UP + 5 + 2 * s):
                                high_part(before, units_before, c)
                            act.wait_ge(chunks, before + SPLIT_SLOTS + 2 * U_UP + 2 * s + 2)
                            act.wait_ge(conv_done, 2 * pair)
                            row = f * FH + i + s * FT
                            hv = dv[s]
                            act.activation(conv_out[:, bass.ds(row, 1), :].rearrange("p a (b n) -> p (a b) n", n=2),
                                           hv[:, 448:576].rearrange("p (b n) -> p b n", n=64)[:, :, 62:64], ACT.Copy).then_inc(conv_rows, 1)
                            act.activation(hb[:, s, 2:514], hv[:, 0:512], ACT.Copy)
                            act.activation(hb[:, s, 516:580], hv[:, 512:576], ACT.Copy).then_inc(dfree[s], 1)
                            act.activation(hb[:, s, 514:516], pr[:, bass.ds(R_SS + 2 * (l * 2 * FT + f * FH + i + s * FT), 2)], ACT.Copy).then_inc(hb_ready, 1)
                        act.wait_ge(conv_done, 2 * pair + 1)
                        act.activation(cv[:, 0, :], cv[:, 0, :], ACT.Silu).then_inc(silu_done, 1)
                        act.wait_ge(act_ready, pair + 1)
                        act.activation(ah[:, bass.ds(i, 1), :].rearrange("p a n -> p (a n)"), at[:], ACT.Copy).then_inc(ah_ready, 1)
                    for c in range(24):
                        high_part(l * CHUNKS + f * (2 * U_HALF), l * (UNITS // 2) + f * (U_HALF // 2), 2 * U_DOWN + 4 + c)
                act.wait_ge(act_steps, here + steps[0])
                act.sem_inc(act_steps, ACT_STRIDE - steps[0])
            act.preload_act_table_set("natural_log_exp_and_others")
            rsqrt_of(LAYERS, 0, 2 * LAYERS + 1, 2)

        @block.vector
        def _(dve):
            steps = [0]
            split = [0]
            base = [0]

            def step(ins):
                ins.then_inc(dve_steps, 1)
                steps[0] += 1

            def settle():
                dve.wait_ge(dve_steps, base[0] + steps[0])

            def low_part(before, c):
                dve.wait_ge(high_done, before + c + 1)
                dve.tensor_tensor(wl[:, c % SPLIT_SLOTS, :], raw[(c // 2) % 2][:, (c % 2) * 512:(c % 2) * 512 + 512],
                                  wh[:, c % SPLIT_SLOTS, :].bitcast(F32), ALU.subtract).then_inc(low_done, 1)

            def low_parts(l, upto):
                while split[0] <= upto:
                    low_part(l * CHUNKS, split[0])
                    split[0] += 1

            def norm(l, r, gain):
                dve.wait_ge(rstd_ready, l * 2 + r + 1)
                for kk in range(KD):
                    if kk > 1:
                        dve.wait_ge(xl_ready, l * 3 * KD + 2 * r * KD + kk - 1)
                    dve.scalar_tensor_tensor(tmp[:, kk % 2, :], x[:, kk, :], gain(kk), rstd[:], ALU.mult, ALU.mult).then_inc(xt_ready, 1)

            def rope(l, n, tile, d):
                dve.wait_ge(roped, l * 8 + (n + 1 if n else 0))
                dve.wait_ge(perms, l * 7 + n + 1)
                step(dve.tensor_tensor(tmp[:, 0, :], tile, cf[:, C_COS:C_COS + T], ALU.mult))
                dve.tensor_tensor(tmp[:, 1, :], dv[d % 2], cf[:, C_SIN:C_SIN + T], ALU.mult).then_inc(dfree[d % 2], 1)
                settle()
                dve.wait_ge(dfree[d % 2], freed(l, d) + 1)
                dve.tensor_tensor(tile, tmp[:, 0, :], tmp[:, 1, :], ALU.add).then_inc(roped, 1)

            for t_, val in ((fparts, 0.0), (chosen, 0.0)):
                step(dve.memset(t_[:], val))
            settle()
            step(dve.memset(eps[:], EPS))
            step(dve.memset(av[64:P, 4, :], 0.0))
            step(dve.memset(chosen[0:64, 64:128], NEG))
            step(dve.memset(chosen[0:TS, 1344:1408], NEG))
            dve.wait_ge(s_const, 48)
            settle()
            dve.tensor_copy(cb[:], w1[:, 0:M_END]).then_inc(s_bf, 1)
            for c in range(SPLIT_SLOTS):
                low_part(0, c)
            first = steps[0]

            with dve.Fori(0, LAYERS) as l:
                split[0] = SPLIT_SLOTS
                steps[0] = 0
                base[0] = l * DVE_STRIDE + first
                norm(l, 0, lambda kk: pr[:, bass.ds(R_GM + l * KD + kk, 1)])
                low_parts(l, 5)
                low_parts(l, 7)
                dve.wait_ge(xl_ready, l * 3 * KD + KD)
                rope(l, 0, ki, D_PKI)
                dve.wait_ge(roped, l * 8 + 1)
                for s in range(2):
                    for r in range(2):
                        ins = dve.tensor_copy(k2[64 * r:64 * r + 64, s, 0:T], z[64 * s:64 * s + 64, 7, :])
                ins.then_inc(roped, 1)
                low_parts(l, 9)
                rope(l, 1, iq[:, 0, :], D_PIQ0)
                low_parts(l, 11)
                dve.wait_ge(chunks, chunks_done(l, 2 * U_SMALL + 2))
                dve.wait_ge(st_small, 32 * l)
                for a, b, dst, scale in ((0, HD, av, 1.0), (HD, HD + IDX_HEADS, wi, 0.5), (HD + IDX_HEADS, SMALL, cfg, 1.0)):
                    dve.tensor_scalar(dst[:, 0:4, :], ab[:, 0, 0:4 * SMALL].rearrange("p (t n) -> p t n", n=SMALL)[:, :, a:b], scale, None, ALU.mult)
                    ins = dve.tensor_scalar(dst[0:TS, 4, :], ab[64:P, 0, 4 * SMALL + a:4 * SMALL + b], scale, None, ALU.mult)
                ins.then_inc(small_ready, 1)
                rope(l, 2, iq[:, 1, :], D_PIQ1)
                dve.wait_ge(logf_mm, l + 1)
                dve.wait_ge(st_lf, 16 * l)
                bias = pr[0:HEADS, bass.ds(R_BF + l, 1)]
                dve.tensor_scalar(z[0:HEADS, 0, 0:TP], ab[0:HEADS, 1, :], bias, -1.0, ALU.add, ALU.mult)
                dve.tensor_scalar(z[0:HEADS, 0, TP:T], ab[0:HEADS, 2, 0:TS], bias, -1.0, ALU.add, ALU.mult).then_inc(ly_ready, 1)
                step(dve.memset(one8, 1.0))
                dve.wait_ge(lt_ready, l + 1)
                step(dve.scalar_tensor_tensor(spf, ly, 0.0, lt, ALU.max, ALU.add))
                settle()
                dve.tensor_scalar(lfo, spf, -1.0, None, ALU.mult).then_inc(logf_ready, 1)
                dve.wait_ge(past_i, 48 * (l + 1))
                step(dve.tensor_tensor_scan(nf[:, 0:TP], one8, spf[:, 0:TP], 0.0, ALU.mult, ALU.add))
                step(dve.tensor_tensor_scan(nf[:, T:KEYS], one8[:, 0:PAST], clf, 0.0, ALU.mult, ALU.subtract))
                settle()
                step(dve.tensor_tensor_scan(nf[:, TP:T], one8[:, 0:TS], spf[:, TP:T], nf[:, KEYS - 1:KEYS], ALU.mult, ALU.add))
                settle()
                for part in range(3):
                    step(dve.tensor_copy(part16, nf))
                    settle()
                    step(dve.tensor_copy(fparts[32 * part:32 * part + HEADS, :], part16))
                    if part < 2:
                        step(dve.tensor_tensor(nf, nf, part16, ALU.subtract))
                    settle()
                dve.sem_inc(fparts_ready, 1)

                for m in (B, C, A):
                    for j in range(4):
                        d = D_AQ[j] if m == A else D_Q[m] + j
                        low_parts(l, 2 * U_Q[m] + 2 * j + 1 + 4)
                        if m == A and j:
                            rope(l, 2 + j, q[:, j - 1, :], D_AP[j - 1])
                    if m == A:
                        rope(l, 6, q[:, 3, :], D_AP[3])
                    if m == B:
                        for i in range(IDX_HEADS):
                            for s in range(4):
                                dve.wait_ge(relus, l * 16 + 4 * i + s + 1)
                                if s < 3:
                                    a, b, o = I_SEG[s]
                                    src, dst, wt = w1[:, a:b], scores[:, o:o + b - a], wi[:, I_QT[s], i:i + 1]
                                else:
                                    src, dst, wt = w1[0:TS, 1152:1472], scores_s[:], wi[0:TS, 4, i:i + 1]
                                if i:
                                    dve.wait_ge(idx_added, l * 16 + 4 * i + s - 3)
                                    dve.scalar_tensor_tensor(dst, src, wt, dst, ALU.mult, ALU.add).then_inc(idx_added, 1)
                                else:
                                    dve.tensor_scalar(dst, src, wt, None, ALU.mult).then_inc(idx_added, 1)
                        dve.wait_ge(idx_added, l * 16 + 16)
                        for end in (256, 640, 1152):
                            step(dve.memset(scores[0:64, end - 64:end], NEG))
                        settle()
                    if m != A:
                        low_parts(l, 2 * U_K[m] + 7 + 4)
                        low_parts(l, 2 * U_V[m] + 7)
                        dve.wait_ge(chunks, chunks_done(l, 2 * U_V[m] + 8))
                        for t in range(4):
                            dve.tensor_copy(v[:, t, :], ab[:, t, :])
                        dve.tensor_copy(v[0:TS, 4, :], dbank[D_V[m] % 2][64:P, 0:512]).then_inc(dfree[D_V[m] % 2], 1)
                        dve.memset(v[64:P, 4, :], 0.0).then_inc(v_ready, 1)
                        low_parts(l, 2 * U_V[m] + 7 + 4)

                    def top_round(r):
                        segs = [(scores[:, 0:256], top8[:, 0, :]), (scores[:, 256:640], top8[:, 1, :]), (scores[:, 640:1152], top8[:, 2, :])]
                        if r < TOPK_S // 8:
                            segs.append((scores_s[:], top8[0:TS, 3, :]))
                        settle()
                        apart(dve)
                        for sc, t8 in segs:
                            step(dve.max(t8, sc))
                        settle()
                        apart(dve)
                        for sc, t8 in segs:
                            step(dve.match_replace(sc, t8, sc, TAKEN))

                    for h in range(HEADS):
                        n_head = 8 * m + h
                        cg = 2 * U_G[m] + 2 * h
                        rows = slice(64 * (h % 2), 64 * (h % 2) + 64)
                        if m == B:
                            low_parts(l, cg + 3)
                            t3 = l * 3 * HEADS + 3 * h
                            for b, cols in enumerate(B_COLS):
                                dve.wait_ge(soft, t3 + b + 1)
                                seg = w1[:, 512 * b:512 * b + cols]
                                dve.scalar_tensor_tensor(seg, ab[:, b, 0:cols], 0.0, seg, ALU.max, ALU.add).then_inc(sps, 1)
                            low_parts(l, cg + 4)
                            top_round(n_head)
                            low_parts(l, cg + 5)
                        else:
                            hh = n_head - 8
                            t4 = l * 64 + 4 * hh

                            def max_step(s):
                                dve.wait_ge(ss, t4 + s + 1)
                                if s == 0:
                                    dve.reduce_max(nm[:, 0:1], ab[:, 0, 0:128], AX_X, negate=True)
                                    last = dve.reduce_max(nm[:, 1:2], ab[:, 0, 128:512], AX_X, negate=True)
                                elif s == 3:
                                    last = dve.reduce_max(nm[0:TS, 4:5], ab[0:TS, 1, 0:384], AX_X, negate=True)
                                else:
                                    last = dve.reduce_max(nm[:, s + 1:s + 2], ab[:, s % 2, 0:S_SEG[s][1] - S_SEG[s][0]], AX_X, negate=True)
                                last.then_inc(maxes, 1)

                            def scale_step(s):
                                dve.wait_ge(exps, t4 + s + 1)
                                a, b = S_SEG[s]
                                n = TS if s == 3 else P
                                lo, hi = ((0, 2), (2, 3), (3, 4), (4, 5))[s]
                                step(dve.reciprocal(ri[0:n, lo:hi], rs[0:n, lo:hi]))
                                settle()
                                if s == 0:
                                    dve.tensor_scalar(w1[:, 0:128], w1[:, 0:128], ri[:, 0:1], None, ALU.mult)
                                    last = dve.tensor_scalar(w1[:, 128:512], w1[:, 128:512], ri[:, 1:2], None, ALU.mult)
                                else:
                                    last = dve.tensor_scalar(w1[0:n, a:b], w1[0:n, a:b], ri[0:n, lo:hi], None, ALU.mult)
                                last.then_inc(scaled, 1)

                            low_parts(l, cg + 3)
                            max_step(0)
                            max_step(1)
                            scale_step(0)
                            low_parts(l, cg + 4)
                            max_step(2)
                            scale_step(1)
                            scale_step(2)
                            max_step(3)
                            scale_step(3)
                            low_parts(l, cg + 5)
                            if m == C:
                                top_round(n_head)
                        dve.wait_ge(pvs, l * 24 + n_head + 1)
                        dve.tensor_copy(q[rows, h // 2, 0:TP], ab[rows, 3, :])
                        dve.tensor_copy(q[rows, h // 2, TP:T], ab[rows, 2, 448:512]).then_inc(o_ready, 1)

                    if m == C:
                        settle()
                        for src, a in ((scores[:], 128), (scores_s[:, PAST:PAST + TS], 1280), (scores_s[:, 0:PAST], 1408)):
                            n = P if a == 128 else TS
                            ins = dve.tensor_scalar(chosen[0:n, a:a + src.shape[1]], src, -2e38, NEG, ALU.is_gt, ALU.mult)
                        ins.then_inc(chosen_ready, 1)
                    dve.wait_ge(o_ready, l * 24 + 8 * m + 8)
                    if m != A:
                        dve.wait_ge(st_k, 16 * (2 * l + m + 1))
                        dve.wait_ge(st_v, 32 * (2 * l + m + 1))
                    for p in range(4):
                        step(dve.tensor_copy(oh[:, p, :], q[:, p, :]))
                        settle()
                        dve.tensor_tensor(ol[:, p, :], q[:, p, :], oh[:, p, :].bitcast(F32), ALU.subtract).then_inc(o_split, 1)
                    if m == B:
                        dve.wait_ge(st_lf, 16 * (l + 1))
                        dve.wait_ge(st_ki, 16 * (l + 1))
                    for j in range(KD):
                        low_parts(l, 2 * U_BR[m] + j + 4)
                        d = D_BR[m] + j
                        dve.wait_ge(chunks, chunks_done(l, 2 * U_BR[m] + j + 1))
                        dve.wait_ge(gates_ready, l * 24 + 8 * m + j + 1)
                        if m == B:
                            dve.tensor_tensor(z[:, j, :], dv[d % 2], g[:, j, :], ALU.mult).then_inc(dfree[d % 2], 1)
                        else:
                            dve.tensor_tensor(g[:, j, :], dv[d % 2], g[:, j, :], ALU.mult).then_inc(dfree[d % 2], 1)
                            dve.wait_ge(dfree[d % 2], freed(l, d) + 1)
                            ins = dve.tensor_tensor(z[:, j, :], z[:, j, :], g[:, j, :], ALU.add)
                            if m == A:
                                ins.then_inc(z_ready, 1)
                            else:
                                step(ins)
                    if m == C:
                        settle()

                for j in range(KD):
                    low_parts(l, 2 * U_OUT + 2 * j + 1 + 4)
                    d = D_OUT + j
                    dve.wait_ge(chunks, chunks_done(l, 2 * U_OUT + 2 * j + 2))
                    dve.tensor_tensor(x[:, j, :], x[:, j, :], dv[d % 2], ALU.add).then_inc(dfree[d % 2], 1)
                norm(l, 1, lambda kk: pr[:, bass.ds(R_GF + l * KD + kk, 1)])
                step(dve.memset(hb[:, :, 0:2], 0.0))
                settle()
                apart(dve)
                in_layer = steps[0]
                with dve.Fori(0, 2) as f:
                    with dve.Fori(0, FH) as i:
                        before = l * CHUNKS + f * (2 * U_HALF) + 4 * i
                        pair = l * FT + f * FH + i
                        for s in range(2):
                            for c in (2 * U_UP + 4 + 2 * s, 2 * U_UP + 5 + 2 * s):
                                low_part(before, c)
                            row = l * 2 * FT + f * FH + i + s * FT
                            dve.wait_ge(hb_ready, 2 * pair + s + 1)
                            if s == 0:
                                dve.wait_ge(act_ready, pair)
                            now = base[0] + in_layer + f * (4 * FH) + 4 * i
                            dve.tensor_scalar(cv[:, s, :], hb[:, s, 2:T + 4], pr[:, bass.ds(R_CW + CONV * row + 2, 1)],
                                              pr[:, bass.ds(R_CB + row, 1)], ALU.mult, ALU.add).then_inc(dve_steps, 1)
                            dve.wait_ge(dve_steps, now + 2 * s + 1)
                            dve.scalar_tensor_tensor(cv[:, s, :], hb[:, s, 1:T + 3], pr[:, bass.ds(R_CW + CONV * row + 1, 1)],
                                                     cv[:, s, :], ALU.mult, ALU.add).then_inc(dve_steps, 1)
                            dve.wait_ge(dve_steps, now + 2 * s + 2)
                            dve.scalar_tensor_tensor(cv[:, s, :], hb[:, s, 0:T + 2], pr[:, bass.ds(R_CW + CONV * row, 1)],
                                                     cv[:, s, :], ALU.mult, ALU.add).then_inc(conv_done, 1)
                        dve.wait_ge(silu_done, pair + 1)
                        dve.wait_ge(conv_done, 2 * pair + 2)
                        dve.wait_ge(al_ready, pair)
                        dve.tensor_tensor(at[:, 0:TP], cv[:, 0, 0:TP], cv[:, 1, 0:TP], ALU.mult)
                        dve.tensor_tensor(at[:, TP:T], cv[:, 0, TP + 2:T + 2], cv[:, 1, TP + 2:T + 2], ALU.mult).then_inc(act_ready, 1)
                    dve.wait_ge(acc_ready, 1 + 3 * l + 1 + f)
                    for j in range(KD):
                        for c in range(3):
                            low_part(l * CHUNKS + f * (2 * U_HALF), 2 * U_DOWN + 4 + 3 * j + c)
                        dve.wait_ge(chunks, chunks_done(l, 2 * U_DOWN + 3 * j + 3) + f * (2 * U_HALF))
                        d = D_DOWN + j
                        dve.tensor_tensor(x[:, j, :], x[:, j, :], dv[d % 2], ALU.add).then_inc(dfree[d % 2], 1)
                used = in_layer + 2 * (4 * FH)
                assert used < DVE_STRIDE
                dve.wait_ge(dve_steps, base[0] + used)
                dve.sem_inc(dve_steps, DVE_STRIDE - used)
            dve.wait_ge(rstd_ready, 2 * LAYERS + 1)
            for j in range(KD):
                dve.scalar_tensor_tensor(z[:, j, :], x[:, j, :], pr[:, R_GE + j:R_GE + j + 1], rstd[:], ALU.mult, ALU.mult).then_inc(y_ready, 1)

        @block.tensor
        def _(pe):
            def dense(before, lo_wait, c0, d, free_at, rh, rl, kks, chunk_blocks=4):
                pe.wait_ge(dfree[d % 2], free_at)
                for n, kk in enumerate(kks):
                    c = c0 + n // 4
                    if n % 4 == 0:
                        pe.wait_ge(low_done, before + c + 1)
                    lo_wait(kk)
                    a = (n % 4) * P
                    hi_w, lo_w = wh[:, c % SPLIT_SLOTS, a:a + P], wl[:, c % SPLIT_SLOTS, a:a + P]
                    for w_, r_, first, last in ((hi_w, rh, True, False), (hi_w, rl, False, False), (lo_w, rh, False, True)):
                        for half in range(2):
                            ins = pe.matmul(dhalf[d % 2][half], w_, r_[:, kk, HALF * half:HALF * half + HALF],
                                            start=first and n == 0, stop=last and n == len(kks) - 1)
                    if n % 4 == 3 or n == len(kks) - 1:
                        ins.then_inc(chunks, 1)

            def no_wait(kk):
                pass

            def norm_sum(l, d, count):
                pe.wait_ge(acc_ready, count)
                pe.wait_ge(dfree[d % 2], freed(l, d))
                for half in range(2):
                    ins = pe.matmul(dhalf[d % 2][half], cf[:, C_ONE:C_ONE + P], sumsq[:, HALF * half:HALF * half + HALF], start=True, stop=True)
                ins.then_inc(norms, 1)

            def xn_wait(l, r):
                def wait(kk):
                    pe.wait_ge(xl_ready, l * 3 * KD + r * KD + kk + 1)
                return wait

            def project(l, u, d, wait=no_wait):
                dense(l * CHUNKS, wait, 2 * u, d, freed(l, d), xh, xl, range(KD))

            def permute(l, tile, d):
                pe.wait_ge(dfree[d % 2], freed(l, d))
                for half in range(2):
                    ins = pe.matmul(dhalf[d % 2][half], cf[:, C_ROT:C_ROT + P], tile[:, HALF * half:HALF * half + HALF], start=True, stop=True)
                ins.then_inc(perms, 1)

            def gate_chunk(l, m, h, s):
                c, d = 2 * U_G[m] + 2 * h + s, D_G[m] + h
                if s == 0:
                    pe.wait_ge(dfree[d % 2], freed(l, d))
                pe.wait_ge(low_done, l * CHUNKS + c + 1)
                for n in range(4):
                    kk = 4 * s + n
                    hi_w, lo_w = wh[:, c % SPLIT_SLOTS, n * P:n * P + P], wl[:, c % SPLIT_SLOTS, n * P:n * P + P]
                    for w_, r_, first, last in ((hi_w, xh, True, False), (hi_w, xl, False, False), (lo_w, xh, False, True)):
                        for half in range(2):
                            ins = pe.matmul(dhalf[d % 2][half], w_, r_[:, kk, HALF * half:HALF * half + HALF],
                                            start=first and kk == 0, stop=last and kk == KD - 1)
                ins.then_inc(chunks, 1)

            def by_token(l, c, kk, n, outs, first, last):
                src, cols, starts = outs
                for t in range(5):
                    a = t * P if t < 4 else T - P
                    o = src(t)
                    for x_, w_, f_, l_ in ((xh, wh, True, False), (xh, wl, False, False), (xl, wh, False, True)):
                        ins = pe.matmul(o, x_[:, kk, a:a + P], w_[:, c % SPLIT_SLOTS, cols:cols + n],
                                        start=first and f_ and starts(t), stop=last and l_, skip_group_check=True)
                return ins

            pe.sem_inc(chunks, SPLIT_SLOTS)
            pe.wait_ge(s_bf, 1)
            with pe.Fori(0, LAYERS) as l:
                norm_sum(l, D_NORM1, 1 + 3 * l)
                project(l, U_KI, D_KI, xn_wait(l, 0))
                project(l, U_IQ, D_IQ0)
                wait_taken(pe, l, D_KI)
                permute(l, ki, D_PKI)
                project(l, U_IQ + 1, D_IQ1)
                wait_taken(pe, l, D_IQ0)
                permute(l, iq[:, 0, :], D_PIQ0)
                for s in range(2):
                    c = 2 * U_SMALL + s
                    pe.wait_ge(low_done, l * CHUNKS + c + 1)
                    if s == 0:
                        pe.wait_ge(o_ready, l * 24)
                    for n in range(4):
                        ins = by_token(l, c, 4 * s + n, SMALL,
                                       (lambda t: ab[:, 0, t * SMALL:(t + 1) * SMALL], n * P, lambda t: t == 0),
                                       s == 0 and n == 0, s == 1 and n == 3)
                    ins.then_inc(chunks, 1)
                wait_taken(pe, l, D_IQ1)
                permute(l, iq[:, 1, :], D_PIQ1)
                pe.wait_ge(small_ready, l + 1)
                for t in range(4):
                    pe.matmul(ab[0:HEADS, 1, t * P:(t + 1) * P], cfg[:, t, :], ident, start=True, stop=True)
                pe.matmul(ab[0:HEADS, 2, 0:TS], cfg[0:TS, 4, :], cf[0:TS, C_ID:C_ID + TS], start=True, stop=True).then_inc(logf_mm, 1)

                for m in (B, C, A):
                    if m != A:
                        for j in range(4):
                            project(l, U_Q[m] + j, D_Q[m] + j)
                    else:
                        for j in range(4):
                            project(l, U_Q[m] + j, D_AQ[j])
                            if j:
                                wait_taken(pe, l, D_AQ[j - 1])
                                permute(l, q[:, j - 1, :], D_AP[j - 1])
                        wait_taken(pe, l, D_AQ[3])
                        permute(l, q[:, 3, :], D_AP[3])
                    if m == B:
                        pe.wait_ge(roped, l * 8 + 4)
                        pe.wait_ge(past_i, 48 * (l + 1))
                        pe.wait_ge(ly_ready, l + 1)
                        for i in range(IDX_HEADS):
                            r = slice(64 * (i % 2), 64 * (i % 2) + 64)
                            for s in range(4):
                                if i:
                                    pe.wait_ge(relus, l * 16 + 4 * i + s - 3)
                                apart(pe)
                                if s < 3:
                                    t = I_QT[s]
                                    ins = pe.matmul(ab[:, s, 0:tile_keys(t)], iq[r, i // 2, t * P:(t + 1) * P], k2[r, 1, 0:tile_keys(t)], start=True, stop=True)
                                else:
                                    pe.matmul(ab[0:TS, 3, 0:PAST], iq[r, i // 2, TP:T], k2[r, 1, T:KEYS], start=True, stop=True)
                                    ins = pe.matmul(ab[0:TS, 3, PAST:PAST + TS], iq[r, i // 2, TP:T], k2[r, 1, TP:T], start=True, stop=True)
                                ins.then_inc(dots, 1)
                    if m != A:
                        for j in range(4):
                            project(l, U_K[m] + j, D_K[m] + j)
                        dvb = dbank[D_V[m] % 2]
                        pe.wait_ge(dfree[D_V[m] % 2], freed(l, D_V[m]))
                        if m == B:
                            pe.wait_ge(relus, l * 16 + 16)
                        else:
                            pe.wait_ge(o_ready, l * 24 + 8)
                        for kk in range(KD):
                            c = 2 * U_V[m] + kk
                            pe.wait_ge(low_done, l * CHUNKS + c + 1)
                            by_token(l, c, kk, 512, (lambda t: ab[:, t, :] if t < 4 else dvb[:, 0:512], 0, lambda t: True),
                                     kk == 0, kk == KD - 1).then_inc(chunks, 1)
                        pe.wait_ge(v_ready, l * 2 + m + 1)
                        pe.wait_ge(past_b if m == B else past_c, 32 * (l + 1))
                    if m == A:
                        pe.wait_ge(roped, l * 8 + 8)
                        pe.wait_ge(chosen_ready, l + 1)
                    else:
                        for j in (2, 3):
                            wait_taken(pe, l, D_K[m] + j)
                    if m == C:
                        pe.wait_ge(fparts_ready, l + 1)

                    for h in range(HEADS):
                        n_head = 8 * m + h
                        r = slice(64 * (h % 2), 64 * (h % 2) + 64)
                        qh = q[r, h // 2, :]
                        kh = k2[r, 0, :] if m == A else k[r, h // 2, :]

                        def val(t):
                            return av[:, t, :] if m == A else v[:, t, h * HD:(h + 1) * HD]

                        if m == B:
                            t3 = l * 3 * HEADS + 3 * h
                            if h:
                                pe.wait_ge(o_ready, l * 24 + n_head)
                            def logits(bank, a, t, first):
                                n = TP - t * P
                                pe.matmul(ab[:, bank, a:a + n], kh[:, t * P:(t + 1) * P], qh[:, t * P:TP], start=first, stop=False, skip_group_check=True)
                                return pe.matmul(ab[:, bank, a:a + P], identb, cb[:, M_SB:M_SB + P], start=False, stop=False, skip_group_check=True)

                            logits(0, 0, 0, True).then_inc(zs, 1)
                            logits(1, 0, 1, True)
                            logits(1, 384, 3, False).then_inc(zs, 1)
                            logits(2, 0, 2, True)
                            for j, a in enumerate((TP, T, T + P)):
                                pe.matmul(ab[:, 2, 256 + 64 * j:320 + 64 * j], kh[:, a:a + P], qh[:, TP:T], start=False, stop=False, skip_group_check=True)
                            pe.matmul(ab[:, 2, 256:320], identb, cb[:, M_SBN:M_SBN + TS], start=False, stop=False, skip_group_check=True).then_inc(zs, 1)
                            gate_chunk(l, m, h, 0)
                            ntri, none = cf[:, C_NTRI:C_NTRI + P], cf[:, C_NONE:C_NONE + P]
                            sp_of = {0: 0, 1: 512, 3: 896, 2: 1024}
                            at_of = {0: (0, 0), 1: (1, 0), 3: (1, 384), 2: (2, 0)}

                            def sums(t, last):
                                bank, a = at_of[t]
                                n = TP - t * P
                                ins = pe.matmul(ab[:, bank, a:a + n], ntri, w1[:, sp_of[t]:sp_of[t] + n], start=False, stop=t == 3, skip_group_check=True)
                                for u in range(t + 1, 4):
                                    n = TP - u * P
                                    b = a + (u - t) * P
                                    ins = pe.matmul(ab[:, bank, b:b + n], none, w1[:, sp_of[u]:sp_of[u] + n], start=False, stop=u == 3, skip_group_check=True)
                                return ins

                            pe.wait_ge(sps, t3 + 3)
                            sums(0, False).then_inc(sufs, 1)
                            sums(1, False)
                            sums(3, True).then_inc(sufs, 1)
                            sums(2, False)
                            for j in range(3):
                                o = ab[:, 2, 256 + 64 * j:320 + 64 * j]
                                ins = pe.matmul(o, ntri, w1[:, 1280 + 64 * j:1344 + 64 * j], start=False, stop=j == 0, skip_group_check=True)
                                for u in ((), (2, 0), (0,))[j]:
                                    ins = pe.matmul(o, none, w1[:, 1280 + 64 * u:1344 + 64 * u], start=False, stop=u == 0, skip_group_check=True)
                            ins.then_inc(sufs, 1)
                            gate_chunk(l, m, h, 1)
                            pe.wait_ge(atts, t3 + 3)
                            for t in range(4):
                                pe.matmul(ab[r, 3, t * P:TP], val(t), w2[:, sp_of[t]:sp_of[t] + TP - t * P], start=t == 0, stop=t == 3, skip_group_check=True)
                            for j in range(3):
                                ins = pe.matmul(ab[r, 2, 448:512], val(4 + j), w2[:, 1280 + 64 * j:1344 + 64 * j], start=j == 0, stop=j == 2, skip_group_check=True)
                            ins.then_inc(pvs, 1)
                            continue

                        hh = n_head - 8
                        t4, t3 = l * 64 + 4 * hh, l * 48 + 3 * hh

                        def score_tile(bank, a, t, first):
                            n = tile_keys(t)
                            pe.matmul(ab[:, bank, a:a + n], qh[:, t * P:(t + 1) * P], kh[:, 0:n], start=first, stop=False, skip_group_check=True)
                            if m == A:
                                c0 = (0, 128, 384, 768)[t]
                                return pe.matmul(ab[:, bank, a:a + n], identb, chosen[:, c0:c0 + n], start=False, stop=True, skip_group_check=True)
                            pe.matmul(ab[:, bank, a:a + n], cb[:, M_SEL + h * P:M_SEL + (h + 1) * P], fparts[:, 0:n], start=False, stop=False, skip_group_check=True)
                            return pe.matmul(ab[:, bank, a + n - P:a + n], identb, cb[:, M_CA:M_CA + P], start=False, stop=True, skip_group_check=True)

                        def score_sample():
                            o = ab[0:TS, 1, :]
                            pe.matmul(o[:, 0:P], qh[:, TP:T], kh[:, TP:TP + P], start=True, stop=False, skip_group_check=True)
                            pe.matmul(o[:, P:P + PAST], qh[:, TP:T], kh[:, T:KEYS], start=False, stop=False, skip_group_check=True)
                            if m == A:
                                return pe.matmul(o[:, 0:384], cb[:, M_ID:M_ID + TS], chosen[:, 1280:1664], start=False, stop=True, skip_group_check=True)
                            sel = cb[:, M_SEL + h * P:M_SEL + h * P + TS]
                            pe.matmul(o[:, 0:P], sel, fparts[:, TP:TP + P], start=False, stop=False, skip_group_check=True)
                            pe.matmul(o[:, P:P + PAST], sel, fparts[:, T:KEYS], start=False, stop=False, skip_group_check=True)
                            return pe.matmul(o[:, 0:P], cb[:, M_ID:M_ID + TS], cb[:, M_CAN:M_CAN + P], start=False, stop=True, skip_group_check=True)

                        if hh:
                            pe.wait_ge(exps, t4 - 1)
                        score_tile(0, 0, 0, True)
                        score_tile(0, 128, 2, False).then_inc(ss, 1)
                        if hh:
                            pe.wait_ge(exps, t4)
                        score_tile(1, 0, 3, True).then_inc(ss, 1)
                        gate_chunk(l, m, h, 0)
                        pe.wait_ge(exps, t4 + 1)
                        score_tile(0, 0, 1, True).then_inc(ss, 1)
                        pe.wait_ge(scaled, t4 + 1)
                        pe.wait_ge(o_ready, l * 24 + n_head)
                        for n in range(4):
                            ins = pe.transpose(ab[:, 2, n * P:(n + 1) * P], w1[:, n * P:(n + 1) * P], ident)
                        ins.then_inc(turned, 1)
                        pe.wait_ge(exps, t4 + 2)
                        apart(pe)
                        score_sample().then_inc(ss, 1)
                        pe.wait_ge(scaled, t4 + 2)
                        pe.wait_ge(pts, t3 + 1)
                        for n in range(4):
                            ins = pe.transpose(ab[:, 2, n * P:(n + 1) * P], w1[:, 512 + n * P:512 + (n + 1) * P], ident)
                        ins.then_inc(turned, 1)
                        gate_chunk(l, m, h, 1)
                        pe.wait_ge(scaled, t4 + 4)
                        pe.wait_ge(pts, t3 + 2)
                        for n in range(2):
                            pe.transpose(ab[:, 2, n * P:(n + 1) * P], w1[:, 1024 + n * P:1024 + (n + 1) * P], ident)
                        for n in range(3):
                            ins = pe.transpose(ab[:, 2, 256 + 64 * n:320 + 64 * n], w1[0:TS, 1280 + n * P:1280 + (n + 1) * P], cf[0:TS, C_ID:C_ID + TS])
                        ins.then_inc(turned, 1)
                        pe.wait_ge(pts, t3 + 3)
                        for t in range(4):
                            pe.matmul(ab[r, 3, t * P:TP], val(t), w2[:, t * 512 + t * P:(t + 1) * 512], start=t == 0, stop=t == 3, skip_group_check=True)
                        for j in range(3):
                            ins = pe.matmul(ab[r, 2, 448:512], val(4 + j), w2[:, 2048 + 64 * j:2112 + 64 * j], start=j == 0, stop=j == 2, skip_group_check=True)
                        ins.then_inc(pvs, 1)

                    for j in range(KD):
                        if j == 0:
                            wait = lambda kk: pe.wait_ge(o_split, l * 12 + 4 * m + kk + 1)
                        else:
                            wait = no_wait
                        d = D_BR[m] + j
                        dense(l * CHUNKS, wait, 2 * U_BR[m] + j, d, freed(l, d), oh, ol, range(4))

                for j in range(KD):
                    project(l, U_OUT + j, D_OUT + j, xn_wait(l, 1) if j == 0 else no_wait)
                norm_sum(l, D_NORM2, 1 + 3 * l + 1)
                with pe.Fori(0, 2) as f:
                    with pe.Fori(0, FH) as i:
                        before = l * CHUNKS + f * (2 * U_HALF) + 4 * i
                        free_at = l * (D_USES // 2) + f * (D_HALF // 2) + i + D_UP // 2
                        for s in range(2):
                            dense(before, xn_wait(l, 2) if s == 0 else no_wait, 2 * U_UP + 2 * s, s, free_at, xh, xl, range(KD))
                    for j in range(KD):
                        d = D_DOWN + j
                        def wait(kk):
                            if j == 0:
                                pe.wait_ge(al_ready, l * FT + f * FH + kk + 1)
                        dense(l * CHUNKS + f * (2 * U_HALF), wait, 2 * U_DOWN + 3 * j, d,
                              freed(l, d) + f * (D_HALF // 2), ah, al, range(FH))
            norm_sum(LAYERS, 0, 1 + 3 * LAYERS)


def _constants(np):
    cf = np.zeros((P, C_END), np.float32)
    i = np.arange(P)
    cf[:, C_ID:C_ID + P] = np.eye(P)
    cf[:, C_NTRI:C_NTRI + P] = -(i[:, None] >= i[None, :]).astype(np.float32)
    cf[:, C_NONE:C_NONE + P] = -1.0
    cf[:, C_ONE:C_ONE + P] = 1.0
    half = ROT // 2
    pos = np.concatenate([np.arange(TP), np.arange(PAST, PAST + TS)]).astype(np.float32)
    freq = (np.float32(500000.0) ** (-np.arange(half, dtype=np.float32) / np.float32(half))).astype(np.float32)
    ang = pos[None, :] * freq[:, None]
    cf[:, C_COS:C_COS + T] = 1.0
    for h in range(2):
        for e in range(half):
            a, b = HD * h + e, HD * h + half + e
            cf[b, C_ROT + a] = 1.0
            cf[a, C_ROT + b] = 1.0
            cf[a, C_COS:C_COS + T] = cf[b, C_COS:C_COS + T] = np.cos(ang[e])
            cf[a, C_SIN:C_SIN + T] = -np.sin(ang[e])
            cf[b, C_SIN:C_SIN + T] = np.sin(ang[e])
    mk = np.zeros((P, M_END), np.float32)
    mk[:, M_ID:M_ID + P] = np.eye(P)
    mk[:, M_SB:M_SB + P] = np.where(i[:, None] >= i[None, :], NEG, 0)
    j = np.arange(TS)
    mk[:, M_SBN:M_SBN + TS] = np.where((i[:, None] >= j[None, :]) | (i[:, None] >= TS), NEG, 0)
    mk[:, M_CA:M_CA + P] = np.where(i[None, :] > i[:, None], NEG, 0)
    mk[:, M_CAN:M_CAN + P] = np.where((i[None, :] > i[:, None]) | (i[None, :] >= TS), NEG, 0)
    for h in range(HEADS):
        for r in (0, 32, 64):
            mk[r + h, M_SEL + h * P:M_SEL + (h + 1) * P] = 1.0
    return cf, mk


def _stream(np, w_in, w_branch, w_gate, w_out, w_up, w_down):
    off = np.cumsum([0, 512, 64, 64, 256, 64, 4, 512, 512, 512, 512, 512, 512, 8])
    aq, ak, avv, iqq, ikk, iw, bq, bk, bv, cq, ck, cvv, cff = [slice(off[n], off[n + 1]) for n in range(13)]
    out = np.zeros((LAYERS * UNITS + 2, P, 1024), np.float32)

    def tiles(wt):
        return wt.reshape(KD, P, -1, P).transpose(2, 1, 0, 3).reshape(-1, P, 1024)

    def blocks(wt):
        kt = wt.shape[0] // P
        return wt.reshape(kt, P, -1, P).transpose(2, 0, 1, 3)

    def units(bl):
        return bl.reshape(-1, 8, P, P).transpose(0, 2, 1, 3).reshape(-1, P, 1024)

    def by_row(wt):
        return wt.reshape(4, 2, P, 512).transpose(0, 2, 1, 3).reshape(4, P, 1024)

    for l in range(LAYERS):
        wi_, u = w_in[l], l * UNITS
        small = np.zeros((D_MODEL, P), np.float32)
        small[:, 0:SMALL] = np.concatenate([wi_[:, avv], wi_[:, iw], wi_[:, cff]], 1)
        out[u + U_KI] = tiles(np.concatenate([wi_[:, ak], wi_[:, ikk]], 1))[0]
        out[u + U_IQ:u + U_IQ + 2] = tiles(wi_[:, iqq])
        out[u + U_SMALL] = tiles(small)[0]
        for m, qq, n in ((B, bq, 1), (C, cq, 2), (A, aq, 0)):
            out[u + U_Q[m]:u + U_Q[m] + 4] = tiles(wi_[:, qq])
            out[u + U_G[m]:u + U_G[m] + 8] = tiles(w_gate[l][:, n * D_MODEL:(n + 1) * D_MODEL])
            out[u + U_BR[m]:u + U_BR[m] + 4] = units(blocks(w_branch[l, n]).reshape(-1, P, P))
        for m, kk, vv in ((B, bk, bv), (C, ck, cvv)):
            out[u + U_K[m]:u + U_K[m] + 4] = tiles(wi_[:, kk])
            out[u + U_V[m]:u + U_V[m] + 4] = by_row(wi_[:, vv])
        out[u + U_OUT:u + U_OUT + 8] = tiles(w_out[l])
        up = tiles(w_up[l])
        down = blocks(w_down[l])
        for f in range(2):
            a = u + U_UP + f * U_HALF
            pairs = out[a:a + 2 * FH].reshape(FH, 2, P, 1024)
            pairs[:, 0] = up[f * FH:(f + 1) * FH]
            pairs[:, 1] = up[FT + f * FH:FT + (f + 1) * FH]
            padded = np.zeros((KD, 12, P, P), np.float32)
            padded[:, 0:FH] = down[:, f * FH:(f + 1) * FH]
            out[a + 2 * FH:a + U_HALF] = units(padded.reshape(-1, P, P))
    return out


def kernel(x_prompt, x_sample, cache_a_k, cache_a_v, cache_a_idx_k, cache_b_k, cache_b_v, cache_c_k, cache_c_v,
           cache_c_logf, state_ffn_conv, norm_mix, w_in, b_f, w_branch, w_gate, w_out, norm_ffn, w_up, conv_w,
           conv_b, w_down, norm_final):
    import numpy as np
    import concourse.bacc as bacc
    from concourse.bass_utils import run_bass_kernel_spmd

    def f(a):
        return np.asarray(a)

    def by_feature(a):
        a = f(a)
        a = a.reshape(a.shape[:-1] + (-1, P))
        return np.moveaxis(a, -1, 0)

    const, masks = _constants(np)
    xs = np.concatenate([f(x_prompt)[0], f(x_sample)[0]], 0)
    par = np.zeros((P, R_END), np.float32)
    par[:, R_GM:R_GF] = by_feature(norm_mix).reshape(P, -1)
    par[:, R_GF:R_GE] = by_feature(norm_ffn).reshape(P, -1)
    par[:, R_GE:R_BF] = by_feature(norm_final).reshape(P, -1)
    par[0:HEADS, R_BF:R_CW] = f(b_f).T
    par[:, R_CW:R_CB] = by_feature(conv_w).transpose(0, 1, 3, 2).reshape(P, -1)
    par[:, R_CB:R_SS] = by_feature(conv_b).reshape(P, -1)
    par[:, R_SS:R_END] = by_feature(f(state_ffn_conv)[:, 0]).transpose(0, 1, 3, 2).reshape(P, -1)
    kt = [f(c)[:, 0].transpose(0, 2, 1) for c in (cache_a_k, cache_a_idx_k)]
    ki_past = np.concatenate([np.stack([kt[0], kt[1]], 2)] * 2, 1)
    bc_k = np.stack([f(c)[:, 0].reshape(LAYERS, PAST, 4, P).transpose(0, 3, 2, 1) for c in (cache_b_k, cache_c_k)], 1)
    bc_v = np.stack([f(c)[:, 0].reshape(LAYERS, PAST, HEADS * HD) for c in (cache_b_v, cache_c_v)], 1)
    ins = {
        "xT": xs.T.reshape(KD, P, T).transpose(1, 0, 2),
        "w": _stream(np, *map(f, (w_in, w_branch, w_gate, w_out, w_up, w_down))),
        "const": const,
        "masks": masks,
        "par": par,
        "ki_past": ki_past,
        "v_past": f(cache_a_v)[:, 0],
        "bc_k_past": bc_k.reshape(2 * LAYERS, P, 4, PAST),
        "bc_v_past": bc_v.reshape(2 * LAYERS, PAST, HEADS * HD),
        "lf_past": f(cache_c_logf)[:, 0].transpose(0, 2, 1),
    }
    outs = {
        "y": (P, KD, T), "o_ki": (LAYERS, P, T), "o_k": (2 * LAYERS, P, 4, T), "o_v": (2 * LAYERS, T, HEADS * HD),
        "o_av": (LAYERS, T, HD), "o_lf": (LAYERS, HEADS, T), "o_conv": (LAYERS, P, 2 * FT, 4),
    }
    nc = bacc.Bacc("TRN2", target_bir_lowering=False, num_devices=1)
    arrays, args = {}, {}
    for name, a in ins.items():
        arrays[f"in_{name}"] = np.ascontiguousarray(a)
        args[name] = nc.dram_tensor(f"in_{name}", a.shape, F32, kind="ExternalInput").ap()
    for name, s in outs.items():
        args[name] = nc.dram_tensor(f"out_{name}", s, F32, kind="ExternalOutput").ap()
    encoder(nc, **args)
    r = run_bass_kernel_spmd(nc, [arrays], core_ids=[0]).results[0]
    yy, ki, kk, vv, avv, lf, cs = (r[f"out_{n}"] for n in outs)
    yy = yy.transpose(2, 1, 0).reshape(T, D_MODEL)
    ki = ki.transpose(0, 2, 1)
    kk = kk.reshape(LAYERS, 2, P, 4, T).transpose(1, 0, 4, 3, 2).reshape(2, LAYERS, T, HEADS, HD)
    vv = vv.reshape(LAYERS, 2, T, HEADS, HD).transpose(1, 0, 2, 3, 4)
    lf = lf.transpose(0, 2, 1)
    cs = cs.transpose(0, 3, 2, 1).reshape(LAYERS, 4, 2 * D_FF)

    def group(a, b, c):
        return [t[:, None, a:b] for t in (ki[:, :, 0:HD], avv, ki[:, :, HD:P], kk[0], vv[0], kk[1], vv[1], lf)] + [cs[:, None, c:c + 2]]

    return tuple(np.ascontiguousarray(t) for t in [yy[None, 0:TP], yy[None, TP:T]] + group(0, TP, 0) + group(TP, T, 2))
```

```python
from contextlib import ExitStack

import concourse.bass as bass
from concourse import mybir

F32 = mybir.dt.float32
F32R = mybir.dt.float32r
BF16 = mybir.dt.bfloat16
ALU = mybir.AluOpType
ACT = mybir.ActivationFunctionType
AX_X = mybir.AxisListType.X

P = 128
D_MODEL = 1024
KD = D_MODEL // P
LAYERS = 2
TP = 512
TS = 64
T = TP + TS
HALF = T // 2
PAST = 256
KEYS = T + PAST
HD = 64
HEADS = 8
IDX_HEADS = 4
D_FF = 2816
FT = D_FF // P
FH = FT // 2
CONV = 3
EPS = 1e-6
NEG = -1e30
TAKEN = -3e38
TOPK_P = 128
TOPK_S = 80
ROT = 16
SMALL = HD + IDX_HEADS + HEADS
QT = TP // P

U_KI, U_IQ, U_SMALL = 0, 1, 3
B, C, A = 0, 1, 2
U_Q = {B: 4, C: 28, A: 52}
U_K = {B: 8, C: 32}
U_V = {B: 12, C: 36}
U_G = {B: 16, C: 40, A: 56}
U_BR = {B: 24, C: 48, A: 64}
U_OUT = 68
U_UP = 76
U_DOWN = U_UP + 2 * FH
U_HALF = 2 * FH + 12
UNITS = U_UP + 2 * U_HALF
CHUNKS = 2 * UNITS
SPLIT_SLOTS = 4
RAW_SLOTS = 2

D_NORM1, D_KI, D_IQ0, D_PKI, D_IQ1, D_PIQ0, D_SMALL, D_PIQ1, D_TURN = range(9)
D_Q = {B: 9, C: 34}
D_K = {B: 13, C: 38}
D_V = {B: 17, C: 42}
D_G = {B: 18, C: 43, A: 67}
D_BR = {B: 26, C: 51, A: 75}
D_AQ, D_AP = (59, 60, 62, 64), (61, 63, 65, 66)
D_OUT = 83
D_NORM2 = 91
D_UP = 92
D_DOWN = D_UP + 2 * FH
D_HALF = 2 * FH + KD
D_USES = D_UP + 2 * D_HALF
assert UNITS % RAW_SLOTS == 0 and CHUNKS % SPLIT_SLOTS == 0 and D_USES % 2 == 0

C_ID, C_NTRI, C_NONE, C_ONE, C_ROT, C_COS, C_SIN, C_END = 0, 128, 256, 384, 512, 640, 640 + T, 640 + 2 * T
M_ID, M_SB, M_SBN, M_CA, M_CAN, M_SEL, M_END = 0, 128, 256, 320, 448, 576, 576 + HEADS * P
R_GM = 0
R_GF = R_GM + LAYERS * KD
R_GE = R_GF + LAYERS * KD
R_BF = R_GE + KD
R_CW = R_BF + LAYERS
R_CB = R_CW + LAYERS * 2 * FT * CONV
R_SS = R_CB + LAYERS * 2 * FT
R_END = R_SS + LAYERS * 2 * FT * 2

B_COLS = (512, 512, 448)
B_ORDER = (1, 2, 0)
V_ORDER = (1, 0, 2, 3)
S_SEG = ((0, 512), (512, 1024), (1024, 1280), (1280, 1664))
I_SEG = ((0, 512, 640), (512, 896, 256), (896, 1152, 0))
I_QT = (3, 2, 1)

DVE_STRIDE, ACT_STRIDE, POOL_STRIDE = 1024, 512, 128


def encoder(nc, xT, w, const, masks, par, ki_past, v_past, bc_k_past, bc_v_past, lf_past,
            y, o_ki, o_k, o_v, o_av, o_lf, o_conv):
    with ExitStack() as ctx:
        def sb(name, shape, dt=F32):
            return ctx.enter_context(nc.sbuf_tensor(name, shape, dt))

        def shared(*groups):
            made, size = [], 0
            for group in groups:
                with ExitStack() as stage:
                    made += [stage.enter_context(nc.sbuf_tensor(n, s, d)) for n, s, d in group]
                words = 0
                for _, s, d in group:
                    n = 1
                    for m in s[1:]:
                        n *= m
                    words += n
                size = max(size, words)
            sb(groups[0][0][0] + "_space", [P, size])
            return made

        x = sb("x", [P, KD, T])
        xh = sb("xh", [P, KD, T], F32R)
        xl = sb("xl", [P, KD, T], F32R)
        q, k, v, g, _, oh, _, ol, ah, al = shared(
            [("q", [P, 4, T], F32), ("k", [P, 4, KEYS], F32), ("v", [P, 7, HEADS * HD], F32),
             ("g", [P, KD, T], F32)],
            [("over_q", [P, 4 * T], F32), ("oh", [P, 4, T], F32R), ("rest_of_k", [P, 4 * PAST], F32),
             ("ol", [P, 4, T], F32R)],
            [("ah", [P, FH, T], F32R), ("al", [P, FH, T], F32R)])
        k2 = sb("k2", [P, 2, KEYS])
        av = sb("av", [P, 7, HD])
        z = sb("z", [P, KD, T])
        w1, w2, _, iq, hb, cv, at = shared(
            [("w1", [P, 1664], F32), ("w2", [P, 2240], F32)],
            [("over_w1", [P, 1664], F32), ("iq", [P, 2, T], F32)],
            [("hb", [P, 2, T + 4], F32), ("cv", [P, 2, T + 2], F32), ("at", [P, T], F32)])
        scores = sb("scores", [P, 1152])
        scores_s = sb("scores_s", [TS, PAST + TS])
        chosen = sb("chosen", [P, 1664], BF16)
        top8 = sb("top8", [P, 4, 8])
        raw = [sb(f"raw{i}", [P, 1024]) for i in range(RAW_SLOTS)]
        wh = sb("wh", [P, SPLIT_SLOTS, 512], F32R)
        wl = sb("wl", [P, SPLIT_SLOTS, 512], F32R)
        tmp = sb("tmp", [P, 2, T])
        rstd = sb("rstd", [P, T])
        sumsq = sb("sumsq", [P, T])
        cf = sb("cf", [P, C_END])
        cb = sb("cb", [P, M_END], BF16)
        pr = sb("pr", [P, R_END])
        fparts = sb("fparts", [P, KEYS], BF16)
        conv_out = sb("conv_out", [P, 2 * FT, 4])
        wi = sb("wi", [P, 5, IDX_HEADS])
        cfg = sb("cfg", [P, 5, HEADS])
        nm = sb("nm", [P, 5])
        rs = sb("rs", [P, 5])
        ri = sb("ri", [P, 5])
        eps = sb("eps", [P, 1])

        ki, small = z[:, 7, :], z[:, 6, :]
        zf = z[:].rearrange("p a b -> p (a b)")
        ly, lt, spf, lfo = z[0:HEADS, 0, :], z[0:HEADS, 1, :], z[0:HEADS, 2, :], z[0:HEADS, 3, :]
        clf, one8, nf = zf[0:HEADS, 4 * T:4 * T + PAST], zf[0:HEADS, 2600:2600 + TP], zf[0:HEADS, 3136:3136 + KEYS]
        part16 = zf[0:HEADS, 4 * T:4 * T + KEYS // 2].bitcast(BF16)

        dbank = [ctx.enter_context(nc.psum_tensor(f"d{i}", [P, 1024], F32)) for i in range(2)]
        ab = ctx.enter_context(nc.psum_tensor("ab", [P, 4, 512], F32))
        dv = [d[:, 512 - HALF:512 + HALF] for d in dbank]
        dhalf = [[d[:, 512 - HALF:512], d[:, 512:512 + HALF]] for d in dbank]

        turned_small = dbank[D_TURN % 2][:, 0:5 * SMALL]

        def sem(name):
            return ctx.enter_context(nc.semaphore(name))

        carrier = sem("carrier")
        s_x, s_const, s_bf = sem("s_x"), sem("s_const"), sem("s_bf")
        landed = [sem(f"landed{i}") for i in range(RAW_SLOTS)]
        high_done, low_done, chunks = sem("high_done"), sem("low_done"), sem("chunks")
        dfree = [sem("dfree0"), sem("dfree1")]
        perms, norms, acc_ready, rstd_ready, xt_ready, xh_ready = map(sem, (
            "perms", "norms", "acc_ready", "rstd_ready", "xt_ready", "xh_ready"))
        xl_ready = [sem("xl_even"), sem("xl_odd")]
        first_squares, last_square = sem("first_squares"), sem("last_square")
        roped = sem("roped")
        past_i, past_b, past_c = sem("past_i"), sem("past_b"), sem("past_c")
        v_taken, v_ready, small_turned = sem("v_taken"), sem("v_ready"), sem("small_turned")
        logf_mm, ly_ready, lt_ready, logf_ready, fparts_ready = map(sem, (
            "logf_mm", "ly_ready", "lt_ready", "logf_ready", "fparts_ready"))
        dots, relus, idx_added, chosen_ready = map(sem, ("dots", "relus", "idx_added", "chosen_ready"))
        zs, soft, sps, sufs, atts = map(sem, ("zs", "soft", "sps", "sufs", "atts"))
        ss, maxes, exps, scaled, turned, pts = map(sem, ("ss", "maxes", "exps", "scaled", "turned", "pts"))
        pvs, o_ready, o_split, gates_ready = map(sem, ("pvs", "o_ready", "o_split", "gates_ready"))
        z_ready, gate_lns = sem("z_ready"), sem("gate_lns")
        hb_ready, conv_done, silu_done, act_ready, ah_ready, al_ready = map(sem, (
            "hb_ready", "conv_done", "silu_done", "act_ready", "ah_ready", "al_ready"))
        st_ki, st_k, st_v, st_small, st_lf, st_conv, st_y = map(sem, (
            "st_ki", "st_k", "st_v", "st_small", "st_lf", "st_conv", "st_y"))
        layer_stored = sem("layer_stored")
        conv_rows, y_ready = sem("conv_rows"), sem("y_ready")
        dve_steps, act_steps, pool_steps = sem("dve_steps"), sem("act_steps"), sem("pool_steps")

        START = 1
        FROM_ONE = (dfree[0], dfree[1], roped, o_ready, conv_done, act_ready, al_ready, layer_stored)

        def chunks_done(l, n):
            return l * CHUNKS + SPLIT_SLOTS + n

        def freed(l, d):
            return START + l * (D_USES // 2) + d // 2

        def wait_low(eng, l, r, kk):
            eng.wait_ge(xl_ready[kk % 2], (l * 3 + r) * (KD // 2) + kk // 2 + 1)

        def wait_taken(eng, l, d):
            eng.wait_ge(dfree[d % 2], freed(l, d) + 1)

        def apart(eng):
            eng.sem_inc(carrier, 1)

        ident, identb = cf[:, C_ID:C_ID + P], cb[:, M_ID:M_ID + P]

        def tile_keys(t):
            return (t + 1) * P

        block = ctx.enter_context(nc.Block())

        @block.sync
        def _(sp):
            sp.dma_start(raw[0][:], w[0]).then_inc(landed[0], 16)
            sp.dma_start(cf[:], const).then_inc(s_const, 16)
            sp.dma_start(pr[:], par).then_inc(s_const, 16)
            sp.dma_start(x[:], xT).then_inc(s_x, 16)
            sp.dma_start(w1[:, 0:M_END], masks).then_inc(s_const, 16)
            sp.dma_start(raw[1][:], w[1]).then_inc(landed[1], 16)
            with sp.Fori(1, (LAYERS * UNITS + 2) // 2) as pair:
                for s in range(2):
                    sp.wait_ge(low_done, 4 * pair + 2 * s - 2)
                    sp.dma_start(raw[s][:], w[bass.ds(2 * pair + s, 1)].rearrange("a p n -> (a p) n"))\
                      .then_inc(landed[s], 16)

        @block.gpsimd
        def _(pool):
            n = [0]

            def square(j, base, ready=None):
                if j == 0:
                    pool.tensor_tensor(sumsq[:], x[:, 0, :], x[:, 0, :], ALU.mult).then_inc(pool_steps, 1)
                    n[0] += 1
                    return
                if j > 1:
                    pool.wait_ge(pool_steps, base + n[0])
                pool.tensor_tensor(rstd[:], x[:, j, :], x[:, j, :], ALU.mult).then_inc(pool_steps, 1)
                n[0] += 1
                pool.wait_ge(pool_steps, base + n[0])
                last = pool.tensor_tensor(sumsq[:], sumsq[:], rstd[:], ALU.add)
                last.then_inc(acc_ready if j == KD - 2 else pool_steps, 1)
                if j < KD - 2:
                    n[0] += 1

            def low_parts(l, r):
                for kk in range(1, KD, 2):
                    pool.wait_ge(xh_ready, l * 3 * KD + r * KD + kk + 1)
                    src = z[:, kk, :] if r == 1 else tmp[:, kk % 2, :]
                    pool.tensor_tensor(xl[:, kk, :], src, xh[:, kk, :].bitcast(F32), ALU.subtract).then_inc(xl_ready[1], 1)

            pool.wait_ge(s_x, 16)
            square(0, 0)
            for j in range(1, KD - 1):
                pool.wait_ge(first_squares, j)
                pool.wait_ge(pool_steps, n[0])
                last = pool.tensor_tensor(sumsq[:], sumsq[:], z[:, j, :], ALU.add)
                last.then_inc(acc_ready if j == KD - 2 else pool_steps, 1)
                if j < KD - 2:
                    n[0] += 1
            first = n[0]
            with pool.Fori(0, LAYERS) as l:
                n[0] = 0
                base = l * POOL_STRIDE + first
                low_parts(l, 0)
                pool.wait_ge(roped, START + l * 8 + 1)
                pool.dma_start(o_ki[bass.ds(l, 1)].rearrange("a p n -> (a p) n"), ki).then_inc(st_ki, 16)
                wait_taken(pool, l, D_TURN)
                pool.dma_start(o_av[bass.ds(l, 1), 0:TP, :].rearrange("a (t p) n -> (a p) t n", p=P), av[:, 0:4, :]).then_inc(st_small, 16)
                pool.dma_start(o_av[bass.ds(l, 1), TP:T, :].rearrange("a p n -> (a p) n"), av[0:TS, 4, :]).then_inc(st_small, 16)
                pool.wait_ge(logf_ready, l + 1)
                pool.dma_start(o_lf[bass.ds(l, 1)].rearrange("a p n -> (a p) n"), lfo).then_inc(st_lf, 16)
                for m in (B, C):
                    for j in (2, 3):
                        wait_taken(pool, l, D_K[m] + j)
                    pool.dma_start(o_k[bass.ds(2 * l + m, 1)].rearrange("a p t n -> (a p) t n"), k[:, :, 0:T]).then_inc(st_k, 16)
                    pool.wait_ge(v_ready, l * 2 + m + 1)
                    apart(pool)
                    ov = o_v[bass.ds(2 * l + m, 1)]
                    pool.dma_start(ov[:, 0:TP, :].rearrange("a (t p) n -> (a p) t n", p=P), v[:, 0:4, :]).then_inc(st_v, 16)
                    pool.dma_start(ov[:, TP:T, :].rearrange("a p n -> (a p) n"), v[0:TS, 4, :]).then_inc(st_v, 16)
                low_parts(l, 1)
                for j in range(KD - 1):
                    wait_taken(pool, l, D_OUT + j)
                    square(j, base)
                low_parts(l, 2)
                per_half = n[0]
                outer = base + n[0]
                with pool.Fori(0, 2) as f:
                    with pool.Fori(0, FH) as i:
                        pool.wait_ge(ah_ready, l * FT + f * FH + i + 1)
                        pool.tensor_tensor(al[:, bass.ds(i, 1), :].rearrange("p a n -> p (a n)"), at[:],
                                           ah[:, bass.ds(i, 1), :].rearrange("p a n -> p (a n)").bitcast(F32),
                                           ALU.subtract).then_inc(al_ready, 1)
                    n[0] = 0
                    for j in range(KD - 1):
                        d = D_DOWN + j
                        pool.wait_ge(dfree[d % 2], freed(l, d) + 1 + f * (D_HALF // 2))
                        square(j, outer + f * per_half)
                assert n[0] == per_half
                pool.wait_ge(pool_steps, base + 3 * per_half)
                pool.sem_inc(pool_steps, POOL_STRIDE - 3 * per_half)
                pool.wait_ge(conv_rows, (l + 1) * 2 * FT)
                pool.dma_start(o_conv[bass.ds(l, 1)].rearrange("a p t n -> (a p) t n"), conv_out[:]).then_inc(st_conv, 16)
                pool.wait_ge(st_small, 32 * (l + 1))
                pool.wait_ge(st_lf, 16 * (l + 1))
                pool.wait_ge(st_conv, 16 * (l + 1))
                pool.sem_inc(layer_stored, 1)
            for j in range(KD):
                pool.wait_ge(y_ready, j + 1)
                pool.dma_start(y[:, j, :], z[:, j, :]).then_inc(st_y, 16)
            for s, count in ((st_ki, LAYERS), (st_small, 2 * LAYERS), (st_lf, LAYERS), (st_k, 2 * LAYERS),
                             (st_v, 4 * LAYERS), (st_conv, LAYERS), (st_y, KD)):
                pool.wait_ge(s, 16 * count)

        @block.scalar
        def _(act):
            steps = [0]
            split = [0]

            def high_parts(l, upto, at_chunk=None):
                while split[0] <= upto:
                    c = split[0]
                    high_part(l * CHUNKS, l * (UNITS // 2), c)
                    split[0] += 1

            def high_part(before, units_before, c):
                v_ = c // 2
                if c % 2 == 0:
                    act.wait_ge(landed[v_ % 2], 16 * (units_before + v_ // 2 + 1))
                act.wait_ge(chunks, before + c + 1)
                act.activation(wh[:, c % SPLIT_SLOTS, :], raw[v_ % 2][:, (c % 2) * 512:(c % 2) * 512 + 512],
                               ACT.Copy).then_inc(high_done, 1)

            def rsqrt_of(l, d, src_count, n_norm):
                act.wait_ge(norms, src_count)
                act.activation(rstd[:], dv[d % 2], ACT.Ln, bias=eps[:], scale=1.0 / D_MODEL).then_inc(dfree[d % 2], 1)
                act.wait_ge(dfree[d % 2], freed(l, d) + 1)
                act.activation(rstd[:], rstd[:], ACT.Exp, scale=-0.5).then_inc(rstd_ready, 1)

            def round_x(l, r, tiles=range(KD)):
                for kk in tiles:
                    if r == 1:
                        act.wait_ge(z_ready, l * KD + kk + 1)
                        src = z[:, kk, :]
                    else:
                        act.wait_ge(xt_ready, l * 2 * KD + (r // 2) * KD + kk + 1)
                        src = tmp[:, kk % 2, :]
                    act.activation(xh[:, kk, :], src, ACT.Copy).then_inc(xh_ready, 1)

            def take(l, d, c_last, dst, scale=1.0):
                high_parts(l, c_last + 4)
                act.wait_ge(chunks, chunks_done(l, c_last + 1))
                return act.activation(dst, dv[d % 2], ACT.Copy, scale=scale)

            def take_query(l, m, j):
                d = D_AQ[j] if m == A else D_Q[m] + j
                take(l, d, 2 * U_Q[m] + 2 * j + 1, q[:, j, :], 0.125).then_inc(dfree[d % 2], 1)

            def gate_soft(l, m, h):
                act.wait_ge(chunks, chunks_done(l, 2 * U_G[m] + 2 * h + 2))
                part = tmp[:, h % 2, :]
                act.activation(part, dv[(D_G[m] + h) % 2], ACT.Abs).then_inc(act_steps, 1)
                steps[0] += 1
                act.wait_ge(act_steps, l * ACT_STRIDE + steps[0])
                act.activation(part, part, ACT.Exp, scale=-1.0).then_inc(act_steps, 1)
                steps[0] += 1
                act.wait_ge(act_steps, l * ACT_STRIDE + steps[0])
                act.activation(part, part, ACT.Ln, bias=1.0).then_inc(gate_lns, 1)

            def gate_exp(l, m, h):
                wait_taken(act, l, D_G[m] + h)
                act.activation(g[:, h, :], g[:, h, :], ACT.Exp).then_inc(gates_ready, 1)

            act.preload_act_table_set("natural_log_exp_and_others")
            act.wait_ge(s_bf, 1)
            for c in range(SPLIT_SLOTS):
                high_part(0, 0, c)
            with act.Fori(0, LAYERS) as l:
                split[0] = SPLIT_SLOTS
                steps[0] = 0
                here = l * ACT_STRIDE
                act.preload_act_table_set("natural_log_exp_and_others")
                rsqrt_of(l, D_NORM1, 2 * l + 1, 0)
                act.dma_start(k2[:, :, T:KEYS], ki_past[bass.ds(l, 1)].rearrange("a p t n -> (a p) t n")).then_inc(past_i, 16)
                act.dma_start(av[:, 5:7, :], v_past[bass.ds(l, 1)].rearrange("a (t p) n -> (a p) t n", p=P)).then_inc(past_i, 16)
                act.dma_start(clf, lf_past[bass.ds(l, 1)].rearrange("a p n -> (a p) n")).then_inc(past_i, 16)
                act.dma_start(k[:, :, T:KEYS], bc_k_past[bass.ds(2 * l, 1)].rearrange("a p t n -> (a p) t n")).then_inc(past_b, 16)
                act.dma_start(v[:, 5:7, :], bc_v_past[bass.ds(2 * l, 1)].rearrange("a (t p) n -> (a p) t n", p=P)).then_inc(past_b, 16)
                round_x(l, 0)
                take(l, D_KI, 1, ki).then_inc(dfree[D_KI % 2], 1)
                take(l, D_IQ0, 3, iq[:, 0, :], 0.125).then_inc(dfree[D_IQ0 % 2], 1)
                take(l, D_IQ1, 5, iq[:, 1, :], 0.125).then_inc(dfree[D_IQ1 % 2], 1)
                take(l, D_SMALL, 7, small).then_inc(dfree[D_SMALL % 2], 1)
                for j in range(2):
                    take_query(l, B, j)
                act.wait_ge(ly_ready, l + 1)
                act.activation(lt, ly, ACT.Abs).then_inc(act_steps, 1)
                steps[0] += 1
                act.wait_ge(act_steps, here + steps[0])
                act.activation(lt, lt, ACT.Exp, scale=-1.0).then_inc(act_steps, 1)
                steps[0] += 1
                act.wait_ge(act_steps, here + steps[0])
                act.activation(lt, lt, ACT.Ln, bias=1.0).then_inc(lt_ready, 1)

                for m in (B, C, A):
                    if m == C:
                        act.wait_ge(chunks, chunks_done(l, 2 * U_BR[B] + KD))
                        act.dma_start(k[:, :, T:KEYS], bc_k_past[bass.ds(2 * l + 1, 1)].rearrange("a p t n -> (a p) t n")).then_inc(past_c, 16)
                        act.dma_start(v[:, 5:7, :], bc_v_past[bass.ds(2 * l + 1, 1)].rearrange("a (t p) n -> (a p) t n", p=P)).then_inc(past_c, 16)
                    for j in range(2 if m == B else 0, 4):
                        take_query(l, m, j)
                    if m == B:
                        for i in range(IDX_HEADS):
                            for s in range(4):
                                act.wait_ge(dots, l * 16 + 4 * i + s + 1)
                                if i:
                                    act.wait_ge(idx_added, l * 16 + 4 * i + s - 3)
                                if s < 3:
                                    a, b, _ = I_SEG[s]
                                    act.activation(w1[:, a:b], ab[:, s, 0:b - a], ACT.Relu).then_inc(relus, 1)
                                else:
                                    act.activation(w1[0:TS, 1152:1472], ab[0:TS, 3, 0:320], ACT.Relu).then_inc(relus, 1)
                    if m != A:
                        for j in range(4):
                            d = D_K[m] + j
                            take(l, d, 2 * U_K[m] + 2 * j + 1, k[:, j, 0:T]).then_inc(dfree[d % 2], 1)
                        high_parts(l, 2 * U_V[m] + 7 + 4)

                    for h in range(HEADS):
                        n_head = 8 * m + h
                        cg = 2 * U_G[m] + 2 * h
                        if m == B:
                            high_parts(l, cg + 3)
                            t3 = l * 3 * HEADS + 3 * h
                            if h:
                                act.wait_ge(sufs, t3)
                            for stage, n, after in ((0, 0, None), (0, 1, None), (1, 0, 1), (0, 2, None), (1, 1, 2), (2, 0, 3), (1, 2, 4), (2, 1, 5), (2, 2, 6)):
                                b = B_ORDER[n]
                                seg = w1[:, 512 * b:512 * b + B_COLS[b]]
                                if stage == 0:
                                    act.wait_ge(zs, t3 + n + 1)
                                    act.activation(seg, ab[:, b, 0:B_COLS[b]], ACT.Abs).then_inc(act_steps, 1)
                                    continue
                                act.wait_ge(act_steps, here + steps[0] + after)
                                if stage == 1:
                                    act.activation(seg, seg, ACT.Exp, scale=-1.0).then_inc(act_steps, 1)
                                else:
                                    act.activation(seg, seg, ACT.Ln, bias=1.0).then_inc(soft, 1)
                            steps[0] += 6
                            high_parts(l, cg + 4)
                            for n, b in enumerate(B_ORDER):
                                act.wait_ge(sufs, t3 + n + 1)
                                if h:
                                    act.wait_ge(pvs, l * 24 + n_head)
                                act.activation(w2[:, 512 * b:512 * b + B_COLS[b]], ab[:, b, 0:B_COLS[b]], ACT.Exp).then_inc(atts, 1)
                            high_parts(l, cg + 5)
                            if h:
                                gate_exp(l, m, h - 1)
                            gate_soft(l, m, h)
                            continue

                        hh = n_head - 8
                        t4, t3 = l * 64 + 4 * hh, l * 48 + 3 * hh

                        def exp_step(s):
                            act.wait_ge(maxes, t4 + s + 1)
                            if hh:
                                act.wait_ge(turned, t3 - 3 + (1, 2, 3, 3)[s])
                            a, b = S_SEG[s]
                            if s == 0:
                                act.activation(w1[:, 0:128], ab[:, 0, 0:128], ACT.Exp, bias=nm[:, 0:1], accum_out=rs[:, 0:1])
                                last = act.activation(w1[:, 128:512], ab[:, 0, 128:512], ACT.Exp, bias=nm[:, 1:2], accum_out=rs[:, 1:2])
                            elif s == 3:
                                last = act.activation(w1[0:TS, a:b], ab[0:TS, 1, 0:384], ACT.Exp, bias=nm[0:TS, 4:5], accum_out=rs[0:TS, 4:5])
                            else:
                                last = act.activation(w1[:, a:b], ab[:, s % 2, 0:b - a], ACT.Exp, bias=nm[:, s + 1:s + 2], accum_out=rs[:, s + 1:s + 2])
                            last.then_inc(exps, 1)

                        def turn_step(s):
                            act.wait_ge(turned, t3 + s + 1)
                            if s == 0:
                                act.wait_ge(pvs, l * 24 + n_head)
                                act.activation(w2[:, 0:128], ab[:, 2, 0:128], ACT.Copy)
                                last = act.activation(w2[:, 0:1536].rearrange("p (t n) -> p t n", n=512)[:, :, 256:384],
                                                      ab[:, 2, 128:512].rearrange("p (t n) -> p t n", n=P), ACT.Copy)
                            elif s == 1:
                                last = act.activation(w2[:, 0:2048].rearrange("p (t n) -> p t n", n=512)[:, :, 384:512],
                                                      ab[:, 2, :].rearrange("p (t n) -> p t n", n=P), ACT.Copy)
                            else:
                                act.activation(w2[:, 0:1024].rearrange("p (t n) -> p t n", n=512)[:, :, 128:256],
                                               ab[:, 2, 0:256].rearrange("p (t n) -> p t n", n=P), ACT.Copy)
                                last = act.activation(w2[:, 2048:2240], ab[:, 2, 256:448], ACT.Copy)
                            last.then_inc(pts, 1)

                        high_parts(l, cg + 3)
                        exp_step(0)
                        exp_step(1)
                        high_parts(l, cg + 4)
                        exp_step(2)
                        turn_step(0)
                        exp_step(3)
                        turn_step(1)
                        high_parts(l, cg + 5)
                        turn_step(2)
                        if h:
                            gate_exp(l, m, h - 1)
                        gate_soft(l, m, h)
                    gate_exp(l, m, HEADS - 1)

                    for j in range(KD):
                        high_parts(l, 2 * U_BR[m] + j + 4)
                        if m == A and j:
                            round_x(l, 1, (j - 1,))

                round_x(l, 1, (KD - 1,))
                high_parts(l, 2 * U_OUT + 2 * KD + 3)
                rsqrt_of(l, D_NORM2, 2 * l + 2, 1)
                round_x(l, 2)

                act.wait_ge(layer_stored, START + l)
                with act.Fori(0, 2) as f:
                    with act.Fori(0, FH) as i:
                        before = l * CHUNKS + f * (2 * U_HALF) + 4 * i
                        units_before = l * (UNITS // 2) + f * (U_HALF // 2) + i
                        pair = l * FT + f * FH + i
                        for s in range(2):
                            for c in (2 * U_UP + 4 + 2 * s, 2 * U_UP + 5 + 2 * s):
                                high_part(before, units_before, c)
                            act.wait_ge(chunks, before + SPLIT_SLOTS + 2 * U_UP + 2 * s + 2)
                            act.wait_ge(conv_done, START + 2 * pair)
                            row = f * FH + i + s * FT
                            hv = dv[s]
                            act.activation(conv_out[:, bass.ds(row, 1), :].rearrange("p a (b n) -> p (a b) n", n=2),
                                           hv[:, 448:576].rearrange("p (b n) -> p b n", n=64)[:, :, 62:64], ACT.Copy).then_inc(conv_rows, 1)
                            act.activation(hb[:, s, 2:514], hv[:, 0:512], ACT.Copy)
                            act.activation(hb[:, s, 516:580], hv[:, 512:576], ACT.Copy).then_inc(dfree[s], 1)
                            act.activation(hb[:, s, 514:516], pr[:, bass.ds(R_SS + 2 * (l * 2 * FT + f * FH + i + s * FT), 2)], ACT.Copy).then_inc(hb_ready, 1)
                        act.wait_ge(conv_done, START + 2 * pair + 1)
                        act.activation(cv[:, 0, :], cv[:, 0, :], ACT.Silu).then_inc(silu_done, 1)
                        act.wait_ge(act_ready, START + pair + 1)
                        act.activation(ah[:, bass.ds(i, 1), :].rearrange("p a n -> p (a n)"), at[:], ACT.Copy).then_inc(ah_ready, 1)
                    for c in range(24):
                        high_part(l * CHUNKS + f * (2 * U_HALF), l * (UNITS // 2) + f * (U_HALF // 2), 2 * U_DOWN + 4 + c)
                act.wait_ge(act_steps, here + steps[0])
                act.sem_inc(act_steps, ACT_STRIDE - steps[0])
            act.preload_act_table_set("natural_log_exp_and_others")
            rsqrt_of(LAYERS, 0, 2 * LAYERS + 1, 2)

        @block.vector
        def _(dve):
            steps = [0]
            split = [0]
            base = [0]

            def step(ins):
                ins.then_inc(dve_steps, 1)
                steps[0] += 1

            def settle():
                dve.wait_ge(dve_steps, base[0] + steps[0])

            def low_part(before, c):
                dve.wait_ge(high_done, before + c + 1)
                dve.tensor_tensor(wl[:, c % SPLIT_SLOTS, :], raw[(c // 2) % 2][:, (c % 2) * 512:(c % 2) * 512 + 512],
                                  wh[:, c % SPLIT_SLOTS, :].bitcast(F32), ALU.subtract).then_inc(low_done, 1)

            def low_parts(l, upto):
                while split[0] <= upto:
                    low_part(l * CHUNKS, split[0])
                    split[0] += 1

            def low_x(l, r, kk, src):
                dve.wait_ge(xh_ready, (l * 3 + r) * KD + kk + 1)
                dve.tensor_tensor(xl[:, kk, :], src, xh[:, kk, :].bitcast(F32), ALU.subtract).then_inc(xl_ready[0], 1)

            def norm(l, r, gain):
                dve.wait_ge(rstd_ready, l * 2 + r + 1)
                for kk in range(KD):
                    if kk > 1:
                        wait_low(dve, l, 2 * r, kk - 2)
                    dve.scalar_tensor_tensor(tmp[:, kk % 2, :], x[:, kk, :], gain(kk), rstd[:], ALU.mult, ALU.mult).then_inc(xt_ready, 1)
                    if kk % 2:
                        low_x(l, 2 * r, kk - 1, tmp[:, 0, :])

            def square_last():
                dve.tensor_tensor(tmp[:, 0, :], x[:, KD - 1, :], x[:, KD - 1, :], ALU.mult).then_inc(last_square, 1)

            def rope(l, n, tile, d):
                dve.wait_ge(roped, START + l * 8 + (n + 1 if n else 0))
                dve.wait_ge(perms, l * 7 + n + 1)
                step(dve.tensor_tensor(tmp[:, 0, :], tile, cf[:, C_COS:C_COS + T], ALU.mult))
                dve.tensor_tensor(tmp[:, 1, :], dv[d % 2], cf[:, C_SIN:C_SIN + T], ALU.mult).then_inc(dfree[d % 2], 1)
                settle()
                dve.wait_ge(dfree[d % 2], freed(l, d) + 1)
                dve.tensor_tensor(tile, tmp[:, 0, :], tmp[:, 1, :], ALU.add).then_inc(roped, 1)

            def split_output(l, m, p):
                dve.wait_ge(o_ready, START + l * 24 + 8 * m + (2 * p + 2 if m == A else HEADS))
                step(dve.tensor_copy(oh[:, p, :], q[:, p, :]))
                settle()
                dve.tensor_tensor(ol[:, p, :], q[:, p, :], oh[:, p, :].bitcast(F32), ALU.subtract).then_inc(o_split, 1)

            dve.wait_ge(s_x, 16)
            for j in range(1, KD - 1):
                dve.tensor_tensor(z[:, j, :], x[:, j, :], x[:, j, :], ALU.mult).then_inc(first_squares, 1)
            square_last()
            for t_, val in ((fparts, 0.0), (chosen, 0.0)):
                step(dve.memset(t_[:], val))
            settle()
            step(dve.memset(eps[:], EPS))
            step(dve.memset(av[64:P, 4, :], 0.0))
            step(dve.memset(chosen[0:64, 64:128], NEG))
            step(dve.memset(chosen[0:TS, 1344:1408], NEG))
            dve.wait_ge(s_const, 48)
            settle()
            dve.tensor_copy(cb[:], w1[:, 0:M_END]).then_inc(s_bf, 1)
            for c in range(SPLIT_SLOTS):
                low_part(0, c)
            first = steps[0]

            with dve.Fori(0, LAYERS) as l:
                split[0] = SPLIT_SLOTS
                steps[0] = 0
                base[0] = l * DVE_STRIDE + first
                norm(l, 0, lambda kk: pr[:, bass.ds(R_GM + l * KD + kk, 1)])
                low_parts(l, 5)
                low_parts(l, 7)
                for kk in (KD - 2, KD - 1):
                    wait_low(dve, l, 0, kk)
                rope(l, 0, ki, D_PKI)
                dve.wait_ge(roped, START + l * 8 + 1)
                for s in range(2):
                    for r in range(2):
                        ins = dve.tensor_copy(k2[64 * r:64 * r + 64, s, 0:T], z[64 * s:64 * s + 64, 7, :])
                ins.then_inc(roped, 1)
                low_parts(l, 9)
                rope(l, 1, iq[:, 0, :], D_PIQ0)
                low_parts(l, 11)
                rope(l, 2, iq[:, 1, :], D_PIQ1)
                dve.wait_ge(small_turned, l + 1)
                dve.wait_ge(layer_stored, START + l)
                for a, b, dst, scale in ((0, HD, av, 1.0), (HD, HD + IDX_HEADS, wi, 0.5), (HD + IDX_HEADS, SMALL, cfg, 1.0)):
                    dve.tensor_scalar(dst[:, 0:4, :], turned_small[:, 0:4 * SMALL].rearrange("p (t n) -> p t n", n=SMALL)[:, :, a:b], scale, None, ALU.mult)
                    ins = dve.tensor_scalar(dst[0:TS, 4, :], turned_small[64:P, 4 * SMALL + a:4 * SMALL + b], scale, None, ALU.mult)
                ins.then_inc(dfree[D_TURN % 2], 1)
                low_parts(l, 15)
                dve.wait_ge(logf_mm, l + 1)
                bias = pr[0:HEADS, bass.ds(R_BF + l, 1)]
                dve.tensor_scalar(z[0:HEADS, 0, 0:TP], ab[0:HEADS, 1, :], bias, -1.0, ALU.add, ALU.mult)
                dve.tensor_scalar(z[0:HEADS, 0, TP:T], ab[0:HEADS, 2, 0:TS], bias, -1.0, ALU.add, ALU.mult).then_inc(ly_ready, 1)
                step(dve.memset(one8, 1.0))
                dve.wait_ge(lt_ready, l + 1)
                step(dve.scalar_tensor_tensor(spf, ly, 0.0, lt, ALU.max, ALU.add))
                settle()
                dve.tensor_scalar(lfo, spf, -1.0, None, ALU.mult).then_inc(logf_ready, 1)
                dve.wait_ge(past_i, 48 * (l + 1))
                step(dve.tensor_tensor_scan(nf[:, 0:TP], one8, spf[:, 0:TP], 0.0, ALU.mult, ALU.add))
                step(dve.tensor_tensor_scan(nf[:, T:KEYS], one8[:, 0:PAST], clf, 0.0, ALU.mult, ALU.subtract))
                settle()
                step(dve.tensor_tensor_scan(nf[:, TP:T], one8[:, 0:TS], spf[:, TP:T], nf[:, KEYS - 1:KEYS], ALU.mult, ALU.add))
                settle()
                for part in range(3):
                    step(dve.tensor_copy(part16, nf))
                    settle()
                    step(dve.tensor_copy(fparts[32 * part:32 * part + HEADS, :], part16))
                    if part < 2:
                        step(dve.tensor_tensor(nf, nf, part16, ALU.subtract))
                    settle()
                dve.sem_inc(fparts_ready, 1)

                for m in (B, C, A):
                    for j in range(4):
                        d = D_AQ[j] if m == A else D_Q[m] + j
                        low_parts(l, 2 * U_Q[m] + 2 * j + 1 + 4)
                        if m == A and j:
                            rope(l, 2 + j, q[:, j - 1, :], D_AP[j - 1])
                    if m == A:
                        rope(l, 6, q[:, 3, :], D_AP[3])
                    if m == B:
                        for i in range(IDX_HEADS):
                            for s in range(4):
                                dve.wait_ge(relus, l * 16 + 4 * i + s + 1)
                                if s < 3:
                                    a, b, o = I_SEG[s]
                                    src, dst, wt = w1[:, a:b], scores[:, o:o + b - a], wi[:, I_QT[s], i:i + 1]
                                else:
                                    src, dst, wt = w1[0:TS, 1152:1472], scores_s[:], wi[0:TS, 4, i:i + 1]
                                if i:
                                    dve.wait_ge(idx_added, l * 16 + 4 * i + s - 3)
                                    dve.scalar_tensor_tensor(dst, src, wt, dst, ALU.mult, ALU.add).then_inc(idx_added, 1)
                                else:
                                    dve.tensor_scalar(dst, src, wt, None, ALU.mult).then_inc(idx_added, 1)
                        dve.wait_ge(idx_added, l * 16 + 16)
                        for end in (256, 640, 1152):
                            step(dve.memset(scores[0:64, end - 64:end], NEG))
                        settle()
                    if m != A:
                        low_parts(l, 2 * U_K[m] + 7 + 4)
                        low_parts(l, 2 * U_V[m] + 7)
                        dve.wait_ge(chunks, chunks_done(l, 2 * U_V[m] + 8))
                        for t in V_ORDER:
                            dve.tensor_copy(v[:, t, :], ab[:, t, :]).then_inc(v_taken, 1)
                        dve.tensor_copy(v[0:TS, 4, :], dbank[D_V[m] % 2][64:P, 0:512]).then_inc(dfree[D_V[m] % 2], 1)
                        dve.memset(v[64:P, 4, :], 0.0).then_inc(v_ready, 1)
                        low_parts(l, 2 * U_V[m] + 7 + 4)

                    def top_round(r):
                        segs = [(scores[:, 0:256], top8[:, 0, :]), (scores[:, 256:640], top8[:, 1, :]), (scores[:, 640:1152], top8[:, 2, :])]
                        if r < TOPK_S // 8:
                            segs.append((scores_s[:], top8[0:TS, 3, :]))
                        settle()
                        apart(dve)
                        for sc, t8 in segs:
                            step(dve.max(t8, sc))
                        settle()
                        apart(dve)
                        for sc, t8 in segs:
                            step(dve.match_replace(sc, t8, sc, TAKEN))

                    for h in range(HEADS):
                        n_head = 8 * m + h
                        cg = 2 * U_G[m] + 2 * h
                        rows = slice(64 * (h % 2), 64 * (h % 2) + 64)
                        if m == B:
                            low_parts(l, cg + 3)
                            t3 = l * 3 * HEADS + 3 * h
                            for n, b in enumerate(B_ORDER):
                                dve.wait_ge(soft, t3 + n + 1)
                                cols = B_COLS[b]
                                seg = w1[:, 512 * b:512 * b + cols]
                                dve.scalar_tensor_tensor(seg, ab[:, b, 0:cols], 0.0, seg, ALU.max, ALU.add).then_inc(sps, 1)
                            low_parts(l, cg + 4)
                            if h < HEADS - 1:
                                top_round(n_head)
                            low_parts(l, cg + 5)
                        else:
                            hh = n_head - 8
                            t4 = l * 64 + 4 * hh

                            def max_step(s):
                                dve.wait_ge(ss, t4 + s + 1)
                                if s == 0:
                                    dve.reduce_max(nm[:, 0:1], ab[:, 0, 0:128], AX_X, negate=True)
                                    last = dve.reduce_max(nm[:, 1:2], ab[:, 0, 128:512], AX_X, negate=True)
                                elif s == 3:
                                    last = dve.reduce_max(nm[0:TS, 4:5], ab[0:TS, 1, 0:384], AX_X, negate=True)
                                else:
                                    last = dve.reduce_max(nm[:, s + 1:s + 2], ab[:, s % 2, 0:S_SEG[s][1] - S_SEG[s][0]], AX_X, negate=True)
                                last.then_inc(maxes, 1)

                            def scale_step(s):
                                dve.wait_ge(exps, t4 + s + 1)
                                a, b = S_SEG[s]
                                n = TS if s == 3 else P
                                lo, hi = ((0, 2), (2, 3), (3, 4), (4, 5))[s]
                                step(dve.reciprocal(ri[0:n, lo:hi], rs[0:n, lo:hi]))
                                settle()
                                if s == 0:
                                    dve.tensor_scalar(w1[:, 0:128], w1[:, 0:128], ri[:, 0:1], None, ALU.mult)
                                    last = dve.tensor_scalar(w1[:, 128:512], w1[:, 128:512], ri[:, 1:2], None, ALU.mult)
                                else:
                                    last = dve.tensor_scalar(w1[0:n, a:b], w1[0:n, a:b], ri[0:n, lo:hi], None, ALU.mult)
                                last.then_inc(scaled, 1)

                            low_parts(l, cg + 3)
                            max_step(0)
                            max_step(1)
                            scale_step(0)
                            low_parts(l, cg + 4)
                            max_step(2)
                            scale_step(1)
                            scale_step(2)
                            max_step(3)
                            scale_step(3)
                            low_parts(l, cg + 5)
                            if m == C and h < HEADS - 1:
                                top_round(n_head)
                        dve.wait_ge(pvs, l * 24 + n_head + 1)
                        dve.tensor_copy(q[rows, h // 2, 0:TP], ab[rows, 3, :])
                        dve.tensor_copy(q[rows, h // 2, TP:T], ab[rows, 2, 448:512]).then_inc(o_ready, 1)
                        if m == A and h % 2:
                            split_output(l, m, h // 2)
                        if m != A and h == HEADS - 1:
                            dve.wait_ge(st_k, 16 * (2 * l + m + 1))
                            dve.wait_ge(st_v, 32 * (2 * l + m + 1))
                            for p in (0, 1):
                                split_output(l, m, p)
                        d = D_G[m] + h
                        dve.wait_ge(gate_lns, l * 24 + n_head + 1)
                        dve.scalar_tensor_tensor(g[:, h, :], dv[d % 2], 0.0, tmp[:, h % 2, :], ALU.min, ALU.subtract).then_inc(dfree[d % 2], 1)
                    if m != A:
                        for p in (2, 3):
                            split_output(l, m, p)

                    if m == B:
                        dve.wait_ge(st_lf, 16 * (l + 1))
                        dve.wait_ge(st_ki, 16 * (l + 1))
                    for j in range(KD):
                        low_parts(l, 2 * U_BR[m] + j + 4)
                        d = D_BR[m] + j
                        dve.wait_ge(chunks, chunks_done(l, 2 * U_BR[m] + j + 1))
                        dve.wait_ge(gates_ready, l * 24 + 8 * m + j + 1)
                        if m == B:
                            dve.tensor_tensor(z[:, j, :], dv[d % 2], g[:, j, :], ALU.mult).then_inc(dfree[d % 2], 1)
                        else:
                            dve.tensor_tensor(g[:, j, :], dv[d % 2], g[:, j, :], ALU.mult).then_inc(dfree[d % 2], 1)
                            dve.wait_ge(dfree[d % 2], freed(l, d) + 1)
                            ins = dve.tensor_tensor(z[:, j, :], z[:, j, :], g[:, j, :], ALU.add)
                            if m == A:
                                ins.then_inc(z_ready, 1)
                                if j % 2:
                                    low_x(l, 1, j - 1, z[:, j - 1, :])
                            else:
                                step(ins)
                    if m != A:
                        top_round(8 * m + 7)
                        settle()
                    if m == C:
                        for src, a in ((scores[:], 128), (scores_s[:, PAST:PAST + TS], 1280), (scores_s[:, 0:PAST], 1408)):
                            n = P if a == 128 else TS
                            ins = dve.tensor_scalar(chosen[0:n, a:a + src.shape[1]], src, -2e38, NEG, ALU.is_gt, ALU.mult)
                        ins.then_inc(chosen_ready, 1)

                for j in range(KD):
                    low_parts(l, 2 * U_OUT + 2 * j + 1 + 4)
                    d = D_OUT + j
                    dve.wait_ge(chunks, chunks_done(l, 2 * U_OUT + 2 * j + 2))
                    dve.tensor_tensor(x[:, j, :], x[:, j, :], dv[d % 2], ALU.add).then_inc(dfree[d % 2], 1)
                wait_taken(dve, l, D_OUT + KD - 1)
                square_last()
                norm(l, 1, lambda kk: pr[:, bass.ds(R_GF + l * KD + kk, 1)])
                step(dve.memset(hb[:, :, 0:2], 0.0))
                settle()
                apart(dve)
                in_layer = steps[0]
                with dve.Fori(0, 2) as f:
                    with dve.Fori(0, FH) as i:
                        before = l * CHUNKS + f * (2 * U_HALF) + 4 * i
                        pair = l * FT + f * FH + i
                        for s in range(2):
                            for c in (2 * U_UP + 4 + 2 * s, 2 * U_UP + 5 + 2 * s):
                                low_part(before, c)
                            row = l * 2 * FT + f * FH + i + s * FT
                            dve.wait_ge(hb_ready, 2 * pair + s + 1)
                            if s == 0:
                                dve.wait_ge(act_ready, START + pair)
                            now = base[0] + in_layer + f * (4 * FH) + 4 * i
                            dve.tensor_scalar(cv[:, s, :], hb[:, s, 2:T + 4], pr[:, bass.ds(R_CW + CONV * row + 2, 1)],
                                              pr[:, bass.ds(R_CB + row, 1)], ALU.mult, ALU.add).then_inc(dve_steps, 1)
                            dve.wait_ge(dve_steps, now + 2 * s + 1)
                            dve.scalar_tensor_tensor(cv[:, s, :], hb[:, s, 1:T + 3], pr[:, bass.ds(R_CW + CONV * row + 1, 1)],
                                                     cv[:, s, :], ALU.mult, ALU.add).then_inc(dve_steps, 1)
                            dve.wait_ge(dve_steps, now + 2 * s + 2)
                            dve.scalar_tensor_tensor(cv[:, s, :], hb[:, s, 0:T + 2], pr[:, bass.ds(R_CW + CONV * row, 1)],
                                                     cv[:, s, :], ALU.mult, ALU.add).then_inc(conv_done, 1)
                        dve.wait_ge(silu_done, pair + 1)
                        dve.wait_ge(conv_done, START + 2 * pair + 2)
                        dve.wait_ge(al_ready, START + pair)
                        dve.tensor_tensor(at[:, 0:TP], cv[:, 0, 0:TP], cv[:, 1, 0:TP], ALU.mult)
                        dve.tensor_tensor(at[:, TP:T], cv[:, 0, TP + 2:T + 2], cv[:, 1, TP + 2:T + 2], ALU.mult).then_inc(act_ready, 1)
                    dve.wait_ge(acc_ready, 1 + 3 * l + 1 + f)
                    for j in range(KD):
                        for c in range(3):
                            low_part(l * CHUNKS + f * (2 * U_HALF), 2 * U_DOWN + 4 + 3 * j + c)
                        dve.wait_ge(chunks, chunks_done(l, 2 * U_DOWN + 3 * j + 3) + f * (2 * U_HALF))
                        d = D_DOWN + j
                        dve.tensor_tensor(x[:, j, :], x[:, j, :], dv[d % 2], ALU.add).then_inc(dfree[d % 2], 1)
                    dve.wait_ge(dfree[d % 2], freed(l, d) + 1 + f * (D_HALF // 2))
                    square_last()
                used = in_layer + 2 * (4 * FH)
                assert used < DVE_STRIDE
                dve.wait_ge(dve_steps, base[0] + used)
                dve.sem_inc(dve_steps, DVE_STRIDE - used)
            dve.wait_ge(rstd_ready, 2 * LAYERS + 1)
            for j in range(KD):
                dve.scalar_tensor_tensor(z[:, j, :], x[:, j, :], pr[:, R_GE + j:R_GE + j + 1], rstd[:], ALU.mult, ALU.mult).then_inc(y_ready, 1)

        @block.tensor
        def _(pe):
            def dense(before, lo_wait, c0, d, free_at, rh, rl, kks, chunk_blocks=4):
                pe.wait_ge(dfree[d % 2], free_at)
                for n, kk in enumerate(kks):
                    c = c0 + n // 4
                    if n % 4 == 0:
                        pe.wait_ge(low_done, before + c + 1)
                    lo_wait(kk)
                    a = (n % 4) * P
                    hi_w, lo_w = wh[:, c % SPLIT_SLOTS, a:a + P], wl[:, c % SPLIT_SLOTS, a:a + P]
                    for w_, r_, first, last in ((hi_w, rh, True, False), (hi_w, rl, False, False), (lo_w, rh, False, True)):
                        for half in range(2):
                            ins = pe.matmul(dhalf[d % 2][half], w_, r_[:, kk, HALF * half:HALF * half + HALF],
                                            start=first and n == 0, stop=last and n == len(kks) - 1)
                    if n % 4 == 3 or n == len(kks) - 1:
                        ins.then_inc(chunks, 1)

            def no_wait(kk):
                pass

            def norm_sum(l, d, count):
                pe.wait_ge(acc_ready, count)
                pe.wait_ge(dfree[d % 2], freed(l, d))
                for src, sq in ((0, sumsq[:]), (1, tmp[:, 0, :])):
                    if src:
                        pe.wait_ge(last_square, count)
                    for half in range(2):
                        ins = pe.matmul(dhalf[d % 2][half], cf[:, C_ONE:C_ONE + P], sq[:, HALF * half:HALF * half + HALF],
                                        start=src == 0, stop=src == 1)
                ins.then_inc(norms, 1)

            def xn_wait(l, r):
                def wait(kk):
                    wait_low(pe, l, r, kk)
                return wait

            def project(l, u, d, wait=no_wait):
                dense(l * CHUNKS, wait, 2 * u, d, freed(l, d), xh, xl, range(KD))

            def permute(l, tile, d):
                pe.wait_ge(dfree[d % 2], freed(l, d))
                for half in range(2):
                    ins = pe.matmul(dhalf[d % 2][half], cf[:, C_ROT:C_ROT + P], tile[:, HALF * half:HALF * half + HALF], start=True, stop=True)
                ins.then_inc(perms, 1)

            def gate_blocks(l, m, h, blocks):
                d = D_G[m] + h
                for kk in blocks:
                    if kk == 0:
                        pe.wait_ge(dfree[d % 2], freed(l, d))
                    c, n = 2 * U_G[m] + 2 * h + kk // 4, kk % 4
                    if n == 0:
                        pe.wait_ge(low_done, l * CHUNKS + c + 1)
                    hi_w, lo_w = wh[:, c % SPLIT_SLOTS, n * P:n * P + P], wl[:, c % SPLIT_SLOTS, n * P:n * P + P]
                    for w_, r_, first, last in ((hi_w, xh, True, False), (hi_w, xl, False, False), (lo_w, xh, False, True)):
                        for half in range(2):
                            ins = pe.matmul(dhalf[d % 2][half], w_, r_[:, kk, HALF * half:HALF * half + HALF],
                                            start=first and kk == 0, stop=last and kk == KD - 1)
                    if n == 3:
                        ins.then_inc(chunks, 1)

            def by_token(l, c, kk, n, outs, first, last):
                src, cols, starts = outs
                for t in range(5):
                    a = t * P if t < 4 else T - P
                    o = src(t)
                    for x_, w_, f_, l_ in ((xh, wh, True, False), (xh, wl, False, False), (xl, wh, False, True)):
                        ins = pe.matmul(o, x_[:, kk, a:a + P], w_[:, c % SPLIT_SLOTS, cols:cols + n],
                                        start=first and f_ and starts(t), stop=last and l_, skip_group_check=True)
                return ins

            pe.sem_inc(chunks, SPLIT_SLOTS)
            for s in FROM_ONE:
                pe.sem_inc(s, START)
            pe.wait_ge(s_bf, 1)
            with pe.Fori(0, LAYERS) as l:
                norm_sum(l, D_NORM1, 1 + 3 * l)
                project(l, U_KI, D_KI, xn_wait(l, 0))
                project(l, U_IQ, D_IQ0)
                wait_taken(pe, l, D_KI)
                permute(l, ki, D_PKI)
                project(l, U_IQ + 1, D_IQ1)
                wait_taken(pe, l, D_IQ0)
                permute(l, iq[:, 0, :], D_PIQ0)
                project(l, U_SMALL, D_SMALL)
                wait_taken(pe, l, D_IQ1)
                permute(l, iq[:, 1, :], D_PIQ1)
                wait_taken(pe, l, D_SMALL)
                for t in range(5):
                    a = t * P if t < 4 else T - P
                    ins = pe.transpose(turned_small[:, t * SMALL:(t + 1) * SMALL], small[0:SMALL, a:a + P], cf[0:SMALL, C_ID:C_ID + SMALL])
                ins.then_inc(small_turned, 1)
                for j in range(2):
                    project(l, U_Q[B] + j, D_Q[B] + j)
                pe.wait_ge(o_ready, START + l * 24)
                wait_taken(pe, l, D_TURN)
                for t in range(4):
                    pe.matmul(ab[0:HEADS, 1, t * P:(t + 1) * P], cfg[:, t, :], ident, start=True, stop=True)
                pe.matmul(ab[0:HEADS, 2, 0:TS], cfg[0:TS, 4, :], cf[0:TS, C_ID:C_ID + TS], start=True, stop=True).then_inc(logf_mm, 1)

                for m in (B, C, A):
                    if m != A:
                        for j in range(2 if m == B else 0, 4):
                            project(l, U_Q[m] + j, D_Q[m] + j)
                    else:
                        for j in range(4):
                            project(l, U_Q[m] + j, D_AQ[j])
                            if j:
                                wait_taken(pe, l, D_AQ[j - 1])
                                permute(l, q[:, j - 1, :], D_AP[j - 1])
                        wait_taken(pe, l, D_AQ[3])
                        permute(l, q[:, 3, :], D_AP[3])
                    if m == B:
                        pe.wait_ge(roped, START + l * 8 + 4)
                        pe.wait_ge(past_i, 48 * (l + 1))
                        pe.wait_ge(ly_ready, l + 1)
                        for i in range(IDX_HEADS):
                            r = slice(64 * (i % 2), 64 * (i % 2) + 64)
                            for s in range(4):
                                if i:
                                    pe.wait_ge(relus, l * 16 + 4 * i + s - 3)
                                apart(pe)
                                if s < 3:
                                    t = I_QT[s]
                                    ins = pe.matmul(ab[:, s, 0:tile_keys(t)], iq[r, i // 2, t * P:(t + 1) * P], k2[r, 1, 0:tile_keys(t)], start=True, stop=True)
                                else:
                                    pe.matmul(ab[0:TS, 3, 0:PAST], iq[r, i // 2, TP:T], k2[r, 1, T:KEYS], start=True, stop=True)
                                    ins = pe.matmul(ab[0:TS, 3, PAST:PAST + TS], iq[r, i // 2, TP:T], k2[r, 1, TP:T], start=True, stop=True)
                                ins.then_inc(dots, 1)
                    if m != A:
                        for j in range(4):
                            project(l, U_K[m] + j, D_K[m] + j)
                        dvb = dbank[D_V[m] % 2]
                        pe.wait_ge(dfree[D_V[m] % 2], freed(l, D_V[m]))
                        if m == B:
                            pe.wait_ge(relus, l * 16 + 16)
                        else:
                            pe.wait_ge(o_ready, START + l * 24 + 8)
                        for kk in range(KD):
                            c = 2 * U_V[m] + kk
                            pe.wait_ge(low_done, l * CHUNKS + c + 1)
                            by_token(l, c, kk, 512, (lambda t: ab[:, t, :] if t < 4 else dvb[:, 0:512], 0, lambda t: True),
                                     kk == 0, kk == KD - 1).then_inc(chunks, 1)
                        pe.wait_ge(past_b if m == B else past_c, 32 * (l + 1))
                    if m == A:
                        pe.wait_ge(chosen_ready, l + 1)
                    else:
                        for j in (2, 3):
                            wait_taken(pe, l, D_K[m] + j)
                    if m == C:
                        pe.wait_ge(fparts_ready, l + 1)

                    def query(h):
                        return q[64 * (h % 2):64 * (h % 2) + 64, h // 2, :]

                    def keys(h):
                        r = slice(64 * (h % 2), 64 * (h % 2) + 64)
                        return k2[r, 0, :] if m == A else k[r, h // 2, :]

                    def score_tile(h, bank, a, t, first):
                        n = tile_keys(t)
                        qh, kh = query(h), keys(h)
                        pe.matmul(ab[:, bank, a:a + n], qh[:, t * P:(t + 1) * P], kh[:, 0:n], start=first, stop=False, skip_group_check=True)
                        if m == A:
                            c0 = (0, 128, 384, 768)[t]
                            return pe.matmul(ab[:, bank, a:a + n], identb, chosen[:, c0:c0 + n], start=False, stop=True, skip_group_check=True)
                        pe.matmul(ab[:, bank, a:a + n], cb[:, M_SEL + h * P:M_SEL + (h + 1) * P], fparts[:, 0:n], start=False, stop=False, skip_group_check=True)
                        return pe.matmul(ab[:, bank, a + n - P:a + n], identb, cb[:, M_CA:M_CA + P], start=False, stop=True, skip_group_check=True)

                    def first_scores(h):
                        if m == A and h % 2 == 0:
                            pe.wait_ge(roped, START + l * 8 + 5 + h // 2)
                        score_tile(h, 0, 0, 0, True)
                        score_tile(h, 0, 128, 2, False).then_inc(ss, 1)

                    for h in range(HEADS):
                        n_head = 8 * m + h
                        r = slice(64 * (h % 2), 64 * (h % 2) + 64)
                        qh, kh = query(h), keys(h)

                        def val(t):
                            return av[:, t, :] if m == A else v[:, t, h * HD:(h + 1) * HD]

                        if m == B:
                            t3 = l * 3 * HEADS + 3 * h
                            def logits(h, bank, a, t, first):
                                n = TP - t * P
                                qh, kh = query(h), keys(h)
                                pe.matmul(ab[:, bank, a:a + n], kh[:, t * P:(t + 1) * P], qh[:, t * P:TP], start=first, stop=False, skip_group_check=True)
                                return pe.matmul(ab[:, bank, a:a + P], identb, cb[:, M_SB:M_SB + P], start=False, stop=False, skip_group_check=True)

                            def first_logits(h):
                                logits(h, 1, 0, 1, True)
                                logits(h, 1, 384, 3, False).then_inc(zs, 1)

                            if h == 0:
                                pe.wait_ge(v_taken, l * 8 + 1)
                                first_logits(0)
                            gate_blocks(l, m, h, range(0, 1))
                            if h:
                                pe.wait_ge(o_ready, START + l * 24 + n_head)
                            else:
                                pe.wait_ge(v_taken, l * 8 + 3)
                            logits(h, 2, 0, 2, True)
                            for j, a in enumerate((TP, T, T + P)):
                                pe.matmul(ab[:, 2, 256 + 64 * j:320 + 64 * j], kh[:, a:a + P], qh[:, TP:T], start=False, stop=False, skip_group_check=True)
                            pe.matmul(ab[:, 2, 256:320], identb, cb[:, M_SBN:M_SBN + TS], start=False, stop=False, skip_group_check=True).then_inc(zs, 1)
                            logits(h, 0, 0, 0, True).then_inc(zs, 1)
                            gate_blocks(l, m, h, range(1, 6))
                            ntri, none = cf[:, C_NTRI:C_NTRI + P], cf[:, C_NONE:C_NONE + P]
                            sp_of = {0: 0, 1: 512, 3: 896, 2: 1024}
                            at_of = {0: (0, 0), 1: (1, 0), 3: (1, 384), 2: (2, 0)}

                            def sums(t):
                                bank, a = at_of[t]
                                n = TP - t * P
                                ins = pe.matmul(ab[:, bank, a:a + n], ntri, w1[:, sp_of[t]:sp_of[t] + n], start=False, stop=t == 3, skip_group_check=True)
                                for u in range(t + 1, 4):
                                    n = TP - u * P
                                    b = a + (u - t) * P
                                    ins = pe.matmul(ab[:, bank, b:b + n], none, w1[:, sp_of[u]:sp_of[u] + n], start=False, stop=u == 3, skip_group_check=True)
                                return ins

                            pe.wait_ge(sps, t3 + 2)
                            sums(1)
                            sums(3).then_inc(sufs, 1)
                            sums(2)
                            for j in range(3):
                                o = ab[:, 2, 256 + 64 * j:320 + 64 * j]
                                ins = pe.matmul(o, ntri, w1[:, 1280 + 64 * j:1344 + 64 * j], start=False, stop=j == 0, skip_group_check=True)
                                for u in ((), (2, 0), (0,))[j]:
                                    ins = pe.matmul(o, none, w1[:, 1280 + 64 * u:1344 + 64 * u], start=False, stop=u == 0, skip_group_check=True)
                            ins.then_inc(sufs, 1)
                            pe.wait_ge(sps, t3 + 3)
                            sums(0).then_inc(sufs, 1)
                            gate_blocks(l, m, h, range(6, 8))
                            if h < HEADS - 1:
                                pe.wait_ge(atts, t3 + 1)
                                first_logits(h + 1)
                            pe.wait_ge(atts, t3 + 3)
                            if h == 0:
                                pe.wait_ge(v_ready, l * 2 + m + 1)
                            for t in range(4):
                                pe.matmul(ab[r, 3, t * P:TP], val(t), w2[:, sp_of[t]:sp_of[t] + TP - t * P], start=t == 0, stop=t == 3, skip_group_check=True)
                            for j in range(3):
                                ins = pe.matmul(ab[r, 2, 448:512], val(4 + j), w2[:, 1280 + 64 * j:1344 + 64 * j], start=j == 0, stop=j == 2, skip_group_check=True)
                            ins.then_inc(pvs, 1)
                            continue

                        hh = n_head - 8
                        t4, t3 = l * 64 + 4 * hh, l * 48 + 3 * hh

                        def score_sample():
                            o = ab[0:TS, 1, :]
                            pe.matmul(o[:, 0:P], qh[:, TP:T], kh[:, TP:TP + P], start=True, stop=False, skip_group_check=True)
                            pe.matmul(o[:, P:P + PAST], qh[:, TP:T], kh[:, T:KEYS], start=False, stop=False, skip_group_check=True)
                            if m == A:
                                return pe.matmul(o[:, 0:384], cb[:, M_ID:M_ID + TS], chosen[:, 1280:1664], start=False, stop=True, skip_group_check=True)
                            sel = cb[:, M_SEL + h * P:M_SEL + h * P + TS]
                            pe.matmul(o[:, 0:P], sel, fparts[:, TP:TP + P], start=False, stop=False, skip_group_check=True)
                            pe.matmul(o[:, P:P + PAST], sel, fparts[:, T:KEYS], start=False, stop=False, skip_group_check=True)
                            return pe.matmul(o[:, 0:P], cb[:, M_ID:M_ID + TS], cb[:, M_CAN:M_CAN + P], start=False, stop=True, skip_group_check=True)

                        if h == 0:
                            if m == C:
                                pe.wait_ge(v_taken, l * 8 + 6)
                            else:
                                pe.wait_ge(exps, t4 - 1)
                            first_scores(0)
                        if hh:
                            pe.wait_ge(exps, t4)
                        score_tile(h, 1, 0, 3, True).then_inc(ss, 1)
                        gate_blocks(l, m, h, range(0, 3))
                        if m == C and h == 0:
                            pe.wait_ge(v_ready, l * 2 + m + 1)
                        pe.wait_ge(exps, t4 + 1)
                        score_tile(h, 0, 0, 1, True).then_inc(ss, 1)
                        gate_blocks(l, m, h, range(3, 5))
                        pe.wait_ge(scaled, t4 + 1)
                        pe.wait_ge(o_ready, START + l * 24 + n_head)
                        for n in range(4):
                            ins = pe.transpose(ab[:, 2, n * P:(n + 1) * P], w1[:, n * P:(n + 1) * P], ident)
                        ins.then_inc(turned, 1)
                        pe.wait_ge(exps, t4 + 2)
                        apart(pe)
                        score_sample().then_inc(ss, 1)
                        gate_blocks(l, m, h, range(5, 7))
                        pe.wait_ge(scaled, t4 + 2)
                        pe.wait_ge(pts, t3 + 1)
                        for n in range(4):
                            ins = pe.transpose(ab[:, 2, n * P:(n + 1) * P], w1[:, 512 + n * P:512 + (n + 1) * P], ident)
                        ins.then_inc(turned, 1)
                        gate_blocks(l, m, h, range(7, 8))
                        pe.wait_ge(scaled, t4 + 4)
                        pe.wait_ge(pts, t3 + 2)
                        for n in range(2):
                            pe.transpose(ab[:, 2, n * P:(n + 1) * P], w1[:, 1024 + n * P:1024 + (n + 1) * P], ident)
                        for n in range(3):
                            ins = pe.transpose(ab[:, 2, 256 + 64 * n:320 + 64 * n], w1[0:TS, 1280 + n * P:1280 + (n + 1) * P], cf[0:TS, C_ID:C_ID + TS])
                        ins.then_inc(turned, 1)
                        if h < HEADS - 1:
                            pe.wait_ge(exps, t4 + 3)
                            first_scores(h + 1)
                        pe.wait_ge(pts, t3 + 3)
                        for t in range(4):
                            pe.matmul(ab[r, 3, t * P:TP], val(t), w2[:, t * 512 + t * P:(t + 1) * 512], start=t == 0, stop=t == 3, skip_group_check=True)
                        for j in range(3):
                            ins = pe.matmul(ab[r, 2, 448:512], val(4 + j), w2[:, 2048 + 64 * j:2112 + 64 * j], start=j == 0, stop=j == 2, skip_group_check=True)
                        ins.then_inc(pvs, 1)

                    for j in range(KD):
                        if j == 0:
                            wait = lambda kk: pe.wait_ge(o_split, l * 12 + 4 * m + kk + 1)
                        else:
                            wait = no_wait
                        d = D_BR[m] + j
                        dense(l * CHUNKS, wait, 2 * U_BR[m] + j, d, freed(l, d), oh, ol, range(4))

                for j in range(KD):
                    project(l, U_OUT + j, D_OUT + j, xn_wait(l, 1) if j == 0 else no_wait)
                norm_sum(l, D_NORM2, 1 + 3 * l + 1)
                with pe.Fori(0, 2) as f:
                    with pe.Fori(0, FH) as i:
                        before = l * CHUNKS + f * (2 * U_HALF) + 4 * i
                        free_at = START + l * (D_USES // 2) + f * (D_HALF // 2) + i + D_UP // 2
                        for s in range(2):
                            dense(before, xn_wait(l, 2) if s == 0 else no_wait, 2 * U_UP + 2 * s, s, free_at, xh, xl, range(KD))
                    for j in range(KD):
                        d = D_DOWN + j
                        def wait(kk):
                            if j == 0:
                                pe.wait_ge(al_ready, START + l * FT + f * FH + kk + 1)
                        dense(l * CHUNKS + f * (2 * U_HALF), wait, 2 * U_DOWN + 3 * j, d,
                              freed(l, d) + f * (D_HALF // 2), ah, al, range(FH))
            norm_sum(LAYERS, 0, 1 + 3 * LAYERS)


def _constants(np):
    cf = np.zeros((P, C_END), np.float32)
    i = np.arange(P)
    cf[:, C_ID:C_ID + P] = np.eye(P)
    cf[:, C_NTRI:C_NTRI + P] = -(i[:, None] >= i[None, :]).astype(np.float32)
    cf[:, C_NONE:C_NONE + P] = -1.0
    cf[:, C_ONE:C_ONE + P] = 1.0
    half = ROT // 2
    pos = np.concatenate([np.arange(TP), np.arange(PAST, PAST + TS)]).astype(np.float32)
    freq = (np.float32(500000.0) ** (-np.arange(half, dtype=np.float32) / np.float32(half))).astype(np.float32)
    ang = pos[None, :] * freq[:, None]
    cf[:, C_COS:C_COS + T] = 1.0
    for h in range(2):
        for e in range(half):
            a, b = HD * h + e, HD * h + half + e
            cf[b, C_ROT + a] = 1.0
            cf[a, C_ROT + b] = 1.0
            cf[a, C_COS:C_COS + T] = cf[b, C_COS:C_COS + T] = np.cos(ang[e])
            cf[a, C_SIN:C_SIN + T] = -np.sin(ang[e])
            cf[b, C_SIN:C_SIN + T] = np.sin(ang[e])
    mk = np.zeros((P, M_END), np.float32)
    mk[:, M_ID:M_ID + P] = np.eye(P)
    mk[:, M_SB:M_SB + P] = np.where(i[:, None] >= i[None, :], NEG, 0)
    j = np.arange(TS)
    mk[:, M_SBN:M_SBN + TS] = np.where((i[:, None] >= j[None, :]) | (i[:, None] >= TS), NEG, 0)
    mk[:, M_CA:M_CA + P] = np.where(i[None, :] > i[:, None], NEG, 0)
    mk[:, M_CAN:M_CAN + P] = np.where((i[None, :] > i[:, None]) | (i[None, :] >= TS), NEG, 0)
    for h in range(HEADS):
        for r in (0, 32, 64):
            mk[r + h, M_SEL + h * P:M_SEL + (h + 1) * P] = 1.0
    return cf, mk


def _stream(np, w_in, w_branch, w_gate, w_out, w_up, w_down):
    off = np.cumsum([0, 512, 64, 64, 256, 64, 4, 512, 512, 512, 512, 512, 512, 8])
    aq, ak, avv, iqq, ikk, iw, bq, bk, bv, cq, ck, cvv, cff = [slice(off[n], off[n + 1]) for n in range(13)]
    out = np.zeros((LAYERS * UNITS + 2, P, 1024), np.float32)

    def tiles(wt):
        return wt.reshape(KD, P, -1, P).transpose(2, 1, 0, 3).reshape(-1, P, 1024)

    def blocks(wt):
        kt = wt.shape[0] // P
        return wt.reshape(kt, P, -1, P).transpose(2, 0, 1, 3)

    def units(bl):
        return bl.reshape(-1, 8, P, P).transpose(0, 2, 1, 3).reshape(-1, P, 1024)

    def by_row(wt):
        return wt.reshape(4, 2, P, 512).transpose(0, 2, 1, 3).reshape(4, P, 1024)

    for l in range(LAYERS):
        wi_, u = w_in[l], l * UNITS
        small = np.zeros((D_MODEL, P), np.float32)
        small[:, 0:SMALL] = np.concatenate([wi_[:, avv], wi_[:, iw], wi_[:, cff]], 1)
        out[u + U_KI] = tiles(np.concatenate([wi_[:, ak], wi_[:, ikk]], 1))[0]
        out[u + U_IQ:u + U_IQ + 2] = tiles(wi_[:, iqq])
        out[u + U_SMALL] = tiles(small)[0]
        for m, qq, n in ((B, bq, 1), (C, cq, 2), (A, aq, 0)):
            out[u + U_Q[m]:u + U_Q[m] + 4] = tiles(wi_[:, qq])
            out[u + U_G[m]:u + U_G[m] + 8] = tiles(w_gate[l][:, n * D_MODEL:(n + 1) * D_MODEL])
            out[u + U_BR[m]:u + U_BR[m] + 4] = units(blocks(w_branch[l, n]).reshape(-1, P, P))
        for m, kk, vv in ((B, bk, bv), (C, ck, cvv)):
            out[u + U_K[m]:u + U_K[m] + 4] = tiles(wi_[:, kk])
            out[u + U_V[m]:u + U_V[m] + 4] = by_row(wi_[:, vv])
        out[u + U_OUT:u + U_OUT + 8] = tiles(w_out[l])
        up = tiles(w_up[l])
        down = blocks(w_down[l])
        for f in range(2):
            a = u + U_UP + f * U_HALF
            pairs = out[a:a + 2 * FH].reshape(FH, 2, P, 1024)
            pairs[:, 0] = up[f * FH:(f + 1) * FH]
            pairs[:, 1] = up[FT + f * FH:FT + (f + 1) * FH]
            padded = np.zeros((KD, 12, P, P), np.float32)
            padded[:, 0:FH] = down[:, f * FH:(f + 1) * FH]
            out[a + 2 * FH:a + U_HALF] = units(padded.reshape(-1, P, P))
    return out


def kernel(x_prompt, x_sample, cache_a_k, cache_a_v, cache_a_idx_k, cache_b_k, cache_b_v, cache_c_k, cache_c_v,
           cache_c_logf, state_ffn_conv, norm_mix, w_in, b_f, w_branch, w_gate, w_out, norm_ffn, w_up, conv_w,
           conv_b, w_down, norm_final):
    import numpy as np
    import concourse.bacc as bacc
    from concourse.bass_utils import run_bass_kernel_spmd

    def f(a):
        return np.asarray(a)

    def by_feature(a):
        a = f(a)
        a = a.reshape(a.shape[:-1] + (-1, P))
        return np.moveaxis(a, -1, 0)

    const, masks = _constants(np)
    xs = np.concatenate([f(x_prompt)[0], f(x_sample)[0]], 0)
    par = np.zeros((P, R_END), np.float32)
    par[:, R_GM:R_GF] = by_feature(norm_mix).reshape(P, -1)
    par[:, R_GF:R_GE] = by_feature(norm_ffn).reshape(P, -1)
    par[:, R_GE:R_BF] = by_feature(norm_final).reshape(P, -1)
    par[0:HEADS, R_BF:R_CW] = f(b_f).T
    par[:, R_CW:R_CB] = by_feature(conv_w).transpose(0, 1, 3, 2).reshape(P, -1)
    par[:, R_CB:R_SS] = by_feature(conv_b).reshape(P, -1)
    par[:, R_SS:R_END] = by_feature(f(state_ffn_conv)[:, 0]).transpose(0, 1, 3, 2).reshape(P, -1)
    kt = [f(c)[:, 0].transpose(0, 2, 1) for c in (cache_a_k, cache_a_idx_k)]
    ki_past = np.concatenate([np.stack([kt[0], kt[1]], 2)] * 2, 1)
    bc_k = np.stack([f(c)[:, 0].reshape(LAYERS, PAST, 4, P).transpose(0, 3, 2, 1) for c in (cache_b_k, cache_c_k)], 1)
    bc_v = np.stack([f(c)[:, 0].reshape(LAYERS, PAST, HEADS * HD) for c in (cache_b_v, cache_c_v)], 1)
    ins = {
        "xT": xs.T.reshape(KD, P, T).transpose(1, 0, 2),
        "w": _stream(np, *map(f, (w_in, w_branch, w_gate, w_out, w_up, w_down))),
        "const": const,
        "masks": masks,
        "par": par,
        "ki_past": ki_past,
        "v_past": f(cache_a_v)[:, 0],
        "bc_k_past": bc_k.reshape(2 * LAYERS, P, 4, PAST),
        "bc_v_past": bc_v.reshape(2 * LAYERS, PAST, HEADS * HD),
        "lf_past": f(cache_c_logf)[:, 0].transpose(0, 2, 1),
    }
    outs = {
        "y": (P, KD, T), "o_ki": (LAYERS, P, T), "o_k": (2 * LAYERS, P, 4, T), "o_v": (2 * LAYERS, T, HEADS * HD),
        "o_av": (LAYERS, T, HD), "o_lf": (LAYERS, HEADS, T), "o_conv": (LAYERS, P, 2 * FT, 4),
    }
    nc = bacc.Bacc("TRN2", target_bir_lowering=False, num_devices=1)
    arrays, args = {}, {}
    for name, a in ins.items():
        arrays[f"in_{name}"] = np.ascontiguousarray(a)
        args[name] = nc.dram_tensor(f"in_{name}", a.shape, F32, kind="ExternalInput").ap()
    for name, s in outs.items():
        args[name] = nc.dram_tensor(f"out_{name}", s, F32, kind="ExternalOutput").ap()
    encoder(nc, **args)
    r = run_bass_kernel_spmd(nc, [arrays], core_ids=[0]).results[0]
    yy, ki, kk, vv, avv, lf, cs = (r[f"out_{n}"] for n in outs)
    yy = yy.transpose(2, 1, 0).reshape(T, D_MODEL)
    ki = ki.transpose(0, 2, 1)
    kk = kk.reshape(LAYERS, 2, P, 4, T).transpose(1, 0, 4, 3, 2).reshape(2, LAYERS, T, HEADS, HD)
    vv = vv.reshape(LAYERS, 2, T, HEADS, HD).transpose(1, 0, 2, 3, 4)
    lf = lf.transpose(0, 2, 1)
    cs = cs.transpose(0, 3, 2, 1).reshape(LAYERS, 4, 2 * D_FF)

    def group(a, b, c):
        return [t[:, None, a:b] for t in (ki[:, :, 0:HD], avv, ki[:, :, HD:P], kk[0], vv[0], kk[1], vv[1], lf)] + [cs[:, None, c:c + 2]]

    return tuple(np.ascontiguousarray(t) for t in [yy[None, 0:TP], yy[None, TP:T]] + group(0, TP, 0) + group(TP, T, 2))
```
